# Optimizing a Trainium2 kernel written in Bass

```python
import jax, jax.numpy as jnp
from jax import lax
import numpy as np

D_MODEL = 1024
BATCH = 1
SEQ = 1024
DEPTH = 2

N_META = 16
CONV_WIDTH = 4
NORM_EPS = 1e-6
RG_WIDTH = 2 * D_MODEL
RG_BLOCK = 256
RG_BLOCKS = RG_WIDTH // RG_BLOCK
RG_C = 8.0
DN_HEAD_DIM = 128
DN_QK_HEADS = D_MODEL // DN_HEAD_DIM
DN_V_HEADS = 2 * DN_QK_HEADS
DN_QK_WIDTH = DN_QK_HEADS * DN_HEAD_DIM
DN_V_WIDTH = DN_V_HEADS * DN_HEAD_DIM
DN_CONV_CH = 2 * DN_QK_WIDTH + DN_V_WIDTH
DN_PROJ = DN_CONV_CH + DN_V_WIDTH + 4 * DN_V_HEADS
CHUNK = 64
N_A_LAYERS = (DEPTH + 1) // 2
N_B_LAYERS = DEPTH // 2

kernel_name = "hybrid_rglru_gdn_meta_encoder"

def rms_norm(x, w):
    xf = x.astype(jnp.float32)
    y = xf * lax.rsqrt(jnp.mean(xf * xf, axis=-1, keepdims=True) + NORM_EPS)
    return (y * w.astype(jnp.float32)).astype(x.dtype)

def l2_norm(x):
    return x * lax.rsqrt(jnp.sum(x * x, axis=-1, keepdims=True) + NORM_EPS)

def dwconv(x, w):
    k, c = w.shape
    return lax.conv_general_dilated(
        x, w.astype(x.dtype)[:, None, :], window_strides=(1,),
        padding=[((k - 1) // 2, k // 2)],
        dimension_numbers=("NWC", "WIO", "NWC"), feature_group_count=c)

def linear_recurrence(a, b):
    def combine(l, r):
        return l[0] * r[0], r[0] * l[1] + r[1]
    _, h = lax.associative_scan(combine, (a, b), axis=1)
    return h

def rglru_mixer(y, w_in, conv_w, conv_b, gate_w, gate_b, lam, w_out):
    bsz, t, _ = y.shape
    xb, zb = jnp.split(y @ w_in, 2, axis=-1)
    xb = dwconv(xb, conv_w) + conv_b.astype(y.dtype)
    xf = xb.astype(jnp.float32)
    xh = xb.reshape(bsz, t, RG_BLOCKS, RG_BLOCK)
    outs = []
    for d in range(2):
        gates = jnp.einsum("btnc,gncm->gbtnm", xh, gate_w[d].astype(y.dtype)) \
            + gate_b[d][:, None, None].astype(y.dtype)
        r = jax.nn.sigmoid(gates[0].astype(jnp.float32)).reshape(bsz, t, RG_WIDTH)
        i = jax.nn.sigmoid(gates[1].astype(jnp.float32)).reshape(bsz, t, RG_WIDTH)
        log_a = -RG_C * jax.nn.softplus(-lam[d].astype(jnp.float32)) * r
        a = jnp.exp(log_a)
        b = jnp.sqrt(-jnp.expm1(2.0 * log_a)) * (i * xf)
        if d == 1:
            h = jnp.flip(linear_recurrence(jnp.flip(a, 1), jnp.flip(b, 1)), 1)
        else:
            h = linear_recurrence(a, b)
        outs.append(h)
    o = (outs[0] + outs[1]) * jax.nn.silu(zb.astype(jnp.float32))
    return o.astype(y.dtype) @ w_out

def chunk_gated_delta(q, k, v, g, beta):
    c = q.shape[3]
    dv = v.shape[-1]
    incl = jnp.tril(jnp.ones((c, c), dtype=bool))
    strict = jnp.tril(jnp.ones((c, c), dtype=bool), -1)
    gc = jnp.cumsum(g, axis=-1)
    diff = gc[..., :, None] - gc[..., None, :]
    decay = jnp.exp(jnp.where(incl, diff, -jnp.inf))
    kb = k * beta[..., None]
    a_mat = jnp.where(strict, jnp.einsum("bhnid,bhnjd->bhnij", kb, k) * decay, 0.0)
    eye = jnp.eye(c, dtype=q.dtype)
    rhs = jnp.concatenate([v * beta[..., None], kb * jnp.exp(gc)[..., None]], axis=-1)
    sol = lax.linalg.triangular_solve(a_mat + eye, rhs, left_side=True, lower=True,
                                      unit_diagonal=True)
    u, w = sol[..., :dv], sol[..., dv:]
    qk = jnp.einsum("bhnid,bhnjd->bhnij", q, k) * decay
    q_dec = q * jnp.exp(gc)[..., None]
    k_tail = k * jnp.exp(gc[..., -1:] - gc)[..., None]
    g_tot = jnp.exp(gc[..., -1])

    def step(s, inp):
        u_n, w_n, qk_n, qd_n, kt_n, gt_n = inp
        v_new = u_n - jnp.einsum("bhck,bhkv->bhcv", w_n, s)
        o = jnp.einsum("bhck,bhkv->bhcv", qd_n, s) + jnp.einsum("bhcj,bhjv->bhcv", qk_n, v_new)
        s = s * gt_n[..., None, None] + jnp.einsum("bhck,bhcv->bhkv", kt_n, v_new)
        return s, o

    bsz, hh = q.shape[0], q.shape[1]
    s0 = jnp.zeros((bsz, hh, q.shape[-1], dv), q.dtype)
    xs = tuple(jnp.moveaxis(z, 2, 0) for z in (u, w, qk, q_dec, k_tail, g_tot))
    _, o = lax.scan(step, s0, xs)
    return jnp.moveaxis(o, 0, 2)

def delta_direction(q, k, v, g, beta, reverse):
    bsz, t, hh, _ = q.shape
    n_pad = (-t) % CHUNK
    arrs = [q, k, v, g, beta]
    if reverse:
        arrs = [jnp.flip(z, 1) for z in arrs]
    lo, hi = (0, n_pad) if reverse else (n_pad, 0)
    arrs = [jnp.pad(z, [(0, 0), (lo, hi)] + [(0, 0)] * (z.ndim - 2)) for z in arrs]
    tp = t + n_pad
    nc = tp // CHUNK
    qc, kc, vc = [z.reshape(bsz, nc, CHUNK, hh, -1).transpose(0, 3, 1, 2, 4) for z in arrs[:3]]
    gcn, bc = [z.reshape(bsz, nc, CHUNK, hh).transpose(0, 3, 1, 2) for z in arrs[3:]]
    o = chunk_gated_delta(qc, kc, vc, gcn, bc)
    o = o.transpose(0, 2, 3, 1, 4).reshape(bsz, tp, hh, -1)[:, lo:tp - hi]
    return jnp.flip(o, 1) if reverse else o

def deltanet_mixer(y, w_in, conv_w, a_log, dt_bias, norm_w, w_out):
    bsz, t, _ = y.shape
    proj = y @ w_in
    qkv, z, ab = jnp.split(proj, [DN_CONV_CH, DN_CONV_CH + DN_V_WIDTH], axis=-1)
    qkv = jax.nn.silu(dwconv(qkv, conv_w))
    q, k, v = jnp.split(qkv, [DN_QK_WIDTH, 2 * DN_QK_WIDTH], axis=-1)
    rep = DN_V_HEADS // DN_QK_HEADS
    q = l2_norm(q.reshape(bsz, t, DN_QK_HEADS, DN_HEAD_DIM).astype(jnp.float32)) * (DN_HEAD_DIM ** -0.5)
    k = l2_norm(k.reshape(bsz, t, DN_QK_HEADS, DN_HEAD_DIM).astype(jnp.float32))
    q = jnp.repeat(q, rep, axis=2)
    k = jnp.repeat(k, rep, axis=2)
    v = v.reshape(bsz, t, DN_V_HEADS, DN_HEAD_DIM).astype(jnp.float32)
    ab = ab.astype(jnp.float32)
    a_in = ab[..., :2 * DN_V_HEADS].reshape(bsz, t, 2, DN_V_HEADS)
    b_in = ab[..., 2 * DN_V_HEADS:].reshape(bsz, t, 2, DN_V_HEADS)
    g = -jnp.exp(a_log.astype(jnp.float32)) * jax.nn.softplus(a_in + dt_bias.astype(jnp.float32))
    beta = jax.nn.sigmoid(b_in)
    o_f = delta_direction(q, k, v, g[:, :, 0], beta[:, :, 0], reverse=False)
    o_b = delta_direction(q, k, v, g[:, :, 1], beta[:, :, 1], reverse=True)
    o = rms_norm(o_f + o_b, norm_w) * jax.nn.silu(z.reshape(bsz, t, DN_V_HEADS, DN_HEAD_DIM).astype(jnp.float32))
    return o.reshape(bsz, t, DN_V_WIDTH).astype(y.dtype) @ w_out

def setup_inputs(seed: int = 0) -> dict:
    key = jax.random.key(seed)
    ks = jax.random.split(key, 16)
    nrm = jax.random.normal
    f32 = jnp.float32
    a0 = jax.random.uniform(ks[8], (N_A_LAYERS, 2, RG_WIDTH), f32, 0.9, 0.999)
    dt = jax.random.uniform(ks[13], (N_B_LAYERS, 2, DN_V_HEADS), f32, 0.001, 0.1)
    return {
        "x": nrm(ks[0], (BATCH, SEQ, D_MODEL), f32),
        "meta_tokens": nrm(ks[1], (N_META, D_MODEL), f32),
        "norm_w": 1.0 + 0.1 * nrm(ks[2], (DEPTH, 2, D_MODEL), f32),
        "rg_w_in": nrm(ks[3], (N_A_LAYERS, D_MODEL, 2 * RG_WIDTH), f32) * D_MODEL ** -0.5,
        "rg_conv_w": nrm(ks[4], (N_A_LAYERS, CONV_WIDTH, RG_WIDTH), f32) * CONV_WIDTH ** -0.5,
        "rg_conv_b": 0.01 * nrm(ks[5], (N_A_LAYERS, RG_WIDTH), f32),
        "rg_gate_w": nrm(ks[6], (N_A_LAYERS, 2, 2, RG_BLOCKS, RG_BLOCK, RG_BLOCK), f32) * RG_BLOCK ** -0.5,
        "rg_gate_b": 0.1 * nrm(ks[7], (N_A_LAYERS, 2, 2, RG_BLOCKS, RG_BLOCK), f32),
        "rg_lambda": jnp.log(a0) - jnp.log1p(-a0),
        "rg_w_out": nrm(ks[9], (N_A_LAYERS, RG_WIDTH, D_MODEL), f32) * RG_WIDTH ** -0.5,
        "dn_w_in": nrm(ks[10], (N_B_LAYERS, D_MODEL, DN_PROJ), f32) * D_MODEL ** -0.5,
        "dn_conv_w": nrm(ks[11], (N_B_LAYERS, CONV_WIDTH, DN_CONV_CH), f32) * CONV_WIDTH ** -0.5,
        "dn_a_log": jnp.log(jax.random.uniform(ks[12], (N_B_LAYERS, 2, DN_V_HEADS), f32, 1.0, 16.0)),
        "dn_dt_bias": jnp.log(jnp.expm1(dt)),
        "dn_norm_w": 1.0 + 0.1 * nrm(ks[14], (N_B_LAYERS, DN_HEAD_DIM), f32),
        "dn_w_out": nrm(ks[15], (N_B_LAYERS, DN_V_WIDTH, D_MODEL), f32) * DN_V_WIDTH ** -0.5,
    }

def reference(x, meta_tokens, norm_w, rg_w_in, rg_conv_w, rg_conv_b, rg_gate_w, rg_gate_b,
              rg_lambda, rg_w_out, dn_w_in, dn_conv_w, dn_a_log, dn_dt_bias, dn_norm_w, dn_w_out):
    bsz = x.shape[0]
    meta = jnp.broadcast_to(meta_tokens.astype(x.dtype)[None], (bsz, N_META, x.shape[-1]))
    h = jnp.concatenate([meta, x], axis=1)
    for i in range(DEPTH):
        y = rms_norm(h, norm_w[i, 0])
        j = i // 2
        if i % 2 == 0:
            y = rglru_mixer(y, rg_w_in[j], rg_conv_w[j], rg_conv_b[j], rg_gate_w[j],
                            rg_gate_b[j], rg_lambda[j], rg_w_out[j])
        else:
            y = deltanet_mixer(y, dn_w_in[j], dn_conv_w[j], dn_a_log[j], dn_dt_bias[j],
                               dn_norm_w[j], dn_w_out[j])
        h = h + rms_norm(y, norm_w[i, 1])
    return h[:, N_META:]


_drawn_inputs = setup_inputs


def setup_inputs(seed=0):
    import zlib

    import numpy as np

    out = dict(_drawn_inputs(seed))
    spreads = {}
    factors = {}
    for name, (base, spread) in spreads.items():
        noise = np.random.default_rng([zlib.crc32(name.encode()), seed]).standard_normal(out[name].shape)
        drawn = base * np.exp(spread * noise) if base else spread * noise
        out[name] = __import__('jax').numpy.asarray(drawn.astype(out[name].dtype))
    for name, factor in factors.items():
        out[name] = (out[name] * factor).astype(out[name].dtype)
    return out
```

```python
import math
from contextlib import ExitStack

import numpy as np

import concourse.bass as bass
from concourse import mybir

F32 = mybir.dt.float32
F32R = mybir.dt.float32r
ALU = mybir.AluOpType
ACT = mybir.ActivationFunctionType

P = 128
D = 1024
KT = D // P
SEQ, META = 1024, 16
T = SEQ + META
CH = 104
NC = T // CH
PIECES = [(0, 416), (416, 416), (832, 208)]
CPB = 4
W = 2048
WT = W // P
RG_BLOCKS = 8
QK_HEADS = 8
V_HEADS = 16
EPS = 1e-6
LEVELS = 7
UNIT = KT * P

A_CONV, A_GATEB = 0, 64
B_NORM, B_CONVB, B_LAM, B_DNNORM = 0, 32, 48, 80


class Phase(ExitStack):

    def __init__(self, nc):
        super().__init__()
        self.nc, self.sems, self.counters, self.programs = nc, [], [], ExitStack()
        self._passed = []

    def semaphore(self, name):
        self.sems.append(self.enter_context(self.nc.semaphore(name)))
        return self.sems[-1]

    @property
    def passed(self):
        if not self._passed:
            self._passed.append(self.semaphore("passed"))
        return self._passed[0]

    def counter(self, name, per=0, start=1):
        self.counters.append(Sem(self.semaphore(name), per, start))
        return self.counters[-1]

    def block(self):
        if self.counters:
            with self.nc.Block() as block:
                @block.gpsimd
                def _(e):
                    for k in self.counters:
                        e.sem_inc(k.sem, k.start)
        return self.programs.enter_context(self.nc.Block())

    def __exit__(self, *exc):
        self.programs.__exit__(*exc)
        if exc[0] is None:
            with self.nc.Block() as block:
                @block.gpsimd
                def _(e):
                    for sem in self.sems:
                        e.sem_clear(sem)
        return super().__exit__(*exc)


class Sem:

    def __init__(self, sem, per=0, start=1):
        self.sem, self.per, self.start = sem, per, start

    def at(self, n, k):
        return n * self.per + (self.start + k)


def build(nc, x, meta_tokens, norm_w, rg_w_in, rg_conv_w, rg_conv_b, rg_gate_w, rg_gate_b, rg_lambda,
          rg_w_out, dn_w_in, dn_conv_w, dn_a_log, dn_dt_bias, dn_norm_w, dn_w_out, out):
    with ExitStack() as top:
        def sb(stack, name, shape, dt=F32):
            return stack.enter_context(nc.sbuf_tensor(name, shape, dt))

        h_dram = nc.dram_tensor("h_scratch", (KT, P, T), F32, kind="Internal").ap()
        y_dram = nc.dram_tensor("y_scratch", (KT, P, T), F32, kind="Internal").ap()
        o_dram = nc.dram_tensor("o_scratch", (WT, P, T), F32, kind="Internal").ap()
        rows_dram = nc.dram_tensor("rows_scratch", (2, 2 * V_HEADS, T), F32, kind="Internal").ap()

        ps = top.enter_context(nc.psum_tensor("ps", [P, 8, 512], F32))
        c = {
            "ident": sb(top, "ident", [P, P]),
            "ones": sb(top, "ones", [P, P]),
            "upto": sb(top, "upto", [CH, 2, CH]),
            "after": sb(top, "after", [CH, 2, CH]),
            "gram_mask": sb(top, "gram_mask", [CH, 2, 2, CH]),
            "level_mask": sb(top, "level_mask", [CH, LEVELS, 2, P], mybir.dt.bfloat16),
            "par": sb(top, "par", [P, 3, P]),
            "rg_half_c": sb(top, "rg_half_c", [P, 32]),
            "rg_neg_half_c": sb(top, "rg_neg_half_c", [P, 32]),
            "rg_half_gateb": sb(top, "rg_half_gateb", [P, 64]),
            "half_dn_norm": sb(top, "half_dn_norm", [P, 1]),
            "eps": sb(top, "eps", [P, 1]),
            "q_bias": sb(top, "q_bias", [P, 1]),
            "k_bias": sb(top, "k_bias", [P, 1]),
        }
        setup(nc, sb, ps, c, x, meta_tokens, norm_w, rg_conv_w, rg_conv_b, rg_gate_b, rg_lambda,
              dn_conv_w, dn_norm_w, h_dram)
        with ExitStack() as s:
            yhi, ylo = sb(s, "rg_yhi", [P, KT, T], F32R), sb(s, "rg_ylo", [P, KT, T], F32R)
            norms(nc, sb, ps, c, "n0", h_dram, None, 0, 0, yhi, ylo)
            rg_loop(nc, sb, ps, c, yhi, ylo, rg_w_in, rg_gate_w, o_dram)
        out_projection(nc, sb, ps, "rgo", rg_w_out, o_dram, y_dram)
        with ExitStack() as s:
            yhi, ylo = sb(s, "dn_yhi", [P, KT, T], F32R), sb(s, "dn_ylo", [P, KT, T], F32R)
            norms(nc, sb, ps, c, "n1", h_dram, y_dram, 1, 2, yhi, ylo)
            with ExitStack() as s2:
                t = {
                    "g": sb(s2, "g", [CH, 2, NC, 16]), "beta": sb(s2, "beta", [CH, 2, NC, 16]),
                    "eg": sb(s2, "eg", [CH, 2, NC, 16]), "tail": sb(s2, "tail", [CH, 2, NC, 16]),
                    "gt": sb(s2, "gt", [P, 2, NC, 16]),
                }
                dn_tables(nc, sb, ps, c, t, yhi, ylo, dn_w_in, dn_a_log, dn_dt_bias, rows_dram)
                dn_loop(nc, sb, ps, c, t, yhi, ylo, dn_w_in, rows_dram, o_dram)
        out_projection(nc, sb, ps, "dno", dn_w_out, o_dram, y_dram)
        norms(nc, sb, ps, c, "n2", h_dram, y_dram, 3, None, None, None, out)


def setup(nc, sb, ps, c, x, meta_tokens, norm_w, rg_conv_w, rg_conv_b, rg_gate_b, rg_lambda,
          dn_conv_w, dn_norm_w, h_dram):
    with Phase(nc) as s:
        prow = sb(s, "prow", [P, 3, P])
        hrow = sb(s, "hrow", [CH, 2, D])
        ht = sb(s, "ht0", [P, KT, T])
        sem = lambda n: s.semaphore(n)
        par_in, masks, par_t, par_done = sem("par_in"), sem("masks"), sem("par_t"), sem("par_done")
        row_in = [sem("row_in0"), sem("row_in1")]
        ident_ready, row_t, row_free, stored = (
            sem("ident_ready"), sem("row_t"), sem("row_free"), sem("h_stored"))
        block = s.block()

        @block.sync
        def _(e):
            loads = [
                (prow[A_CONV:A_CONV + 64, 0, :], rg_conv_w.rearrange("a j (t p) -> (a j t) p", p=P)),
                (prow[A_GATEB:A_GATEB + 64, 0, :],
                 rg_gate_b.rearrange("a d g n (t p) -> (a d g n t) p", p=P)),
                (prow[B_NORM:B_NORM + 32, 1, :], norm_w.rearrange("a b (k p) -> (a b k) p", p=P)),
                (prow[B_CONVB:B_CONVB + 16, 1, :], rg_conv_b.rearrange("a (t p) -> (a t) p", p=P)),
                (prow[B_LAM:B_LAM + 32, 1, :], rg_lambda.rearrange("a d (t p) -> (a d t) p", p=P)),
                (prow[B_DNNORM:B_DNNORM + 1, 1, :], dn_norm_w),
                (prow[:, 2, :], dn_conv_w.rearrange("a j (t p) -> (a j t) p", p=P)),
            ]
            for dst, src in loads:
                e.dma_start(dst, src).then_inc(par_in, 16)
            for k in range(NC):
                if k >= 2:
                    e.wait_ge(row_t, k - 1)
                if k == 0:
                    e.dma_start(hrow[0:META, 0, :], meta_tokens).then_inc(row_in[0], 16)
                    e.dma_start(hrow[META:CH, 0, :], x[0, 0:CH - META, :]).then_inc(row_in[0], 16)
                else:
                    e.dma_start(hrow[:, k % 2, :], x[0, k * CH - META:(k + 1) * CH - META, :]) \
                        .then_inc(row_in[k % 2], 16)
            e.wait_ge(row_free, NC)
            e.dma_start(h_dram.rearrange("k p t -> p k t"), ht[:, :, :]).then_inc(stored, 16)
            e.wait_ge(stored, 16)

        @block.gpsimd
        def _(e):
            count = [0]

            def then(ins):
                count[0] += 1
                ins.then_inc(masks, 1)
                e.wait_ge(masks, count[0])

            def select(view, op, fill, base, ch, pattern):
                then(e.affine_select(out=view, in_=view, compare_op=op, fill=fill, base=base,
                                     pattern=pattern, channel_multiplier=ch))

            then(e.memset(c["ident"][:, :], 0.0))
            e.affine_select(out=c["ident"][:, :], in_=c["ident"][:, :], compare_op=ALU.not_equal,
                            fill=1.0, base=0, pattern=[[-1, P]], channel_multiplier=1) \
                .then_inc(ident_ready, 1)
            then(e.memset(c["ones"][:, :], 1.0))
            then(e.memset(c["eps"][:, :], EPS))
            then(e.memset(c["q_bias"][:, :], math.log(0.5 / math.sqrt(P))))
            then(e.memset(c["k_bias"][:, :], math.log(0.5)))
            for m in ("upto", "after"):
                then(e.memset(c[m][:, :, :], 1.0))
            select(c["upto"][:, 0, :], ALU.is_ge, 0.0, 0, -1, [[1, CH]])
            select(c["upto"][:, 1, :], ALU.is_ge, 0.0, 0, 1, [[-1, CH]])
            select(c["after"][:, 0, :], ALU.is_gt, 0.0, 0, 1, [[-1, CH]])
            select(c["after"][:, 1, :], ALU.is_gt, 0.0, 0, -1, [[1, CH]])
            gm = c["gram_mask"]
            then(e.memset(gm[:, :, 0, :], -1.0))
            then(e.memset(gm[:, :, 1, :], 1.0))
            select(gm[:, 0, 0, :], ALU.is_gt, 0.0, 0, -1, [[1, CH]])
            select(gm[:, 1, 0, :], ALU.is_gt, 0.0, 0, 1, [[-1, CH]])
            select(gm[:, 0, 1, :], ALU.is_ge, 0.0, 0, -1, [[1, CH]])
            select(gm[:, 1, 1, :], ALU.is_ge, 0.0, 0, 1, [[-1, CH]])
            lm = c["level_mask"]
            then(e.memset(lm[:, :, :, :], 0.0))
            for l in range(LEVELS):
                m = 1 << l
                nb = P // (2 * m)
                v = [lm[:, l, d, :].rearrange("p (b h j) -> p b h j", h=2, j=m)[:, :, d, :] for d in (0, 1)]
                for d in (0, 1):
                    then(e.memset(v[d], 1.0))
                select(v[0], ALU.is_ge, 0.0, -m, 1, [[-2 * m, nb], [0, m]])
                select(v[0], ALU.is_ge, 0.0, 2 * m - 1, -1, [[2 * m, nb], [0, m]])
                select(v[1], ALU.is_ge, 0.0, 0, 1, [[-2 * m, nb], [0, m]])
                select(v[1], ALU.is_ge, 0.0, m - 1, -1, [[2 * m, nb], [0, m]])
                for d in (0, 1):
                    select(lm[:, l, d, :], ALU.not_equal, 1.0, 0, 1, [[-1, P]])

        @block.tensor
        def _(e):
            e.wait_ge(ident_ready, 1)
            e.wait_ge(par_in, 16 * 7)
            for k, rows in enumerate((P, 81, P)):
                ins = e.transpose(ps[:, 6, k * P:k * P + rows], prow[0:rows, k, :],
                                  c["ident"][0:rows, 0:rows])
            ins.then_inc(par_t, 1)
            for k in range(NC):
                slot = k % 2
                e.wait_ge(row_in[slot], 16 * (k // 2 + 1 + (slot == 0)))
                if k >= 2:
                    e.wait_ge(row_free, k - 1)
                for b in range(KT):
                    o = ps[:, 2 * slot + b // 4, (b % 4) * CH:(b % 4 + 1) * CH]
                    ins = e.transpose(o, hrow[:, slot, b * P:(b + 1) * P], c["ident"][0:CH, 0:CH])
                ins.then_inc(row_t, 1)

        @block.vector
        def _(e):
            for k in range(NC):
                e.wait_ge(row_t, k + 1)
                src = ps[:, 2 * (k % 2):2 * (k % 2) + 2, 0:4 * CH].rearrange("p a (b t) -> p a b t", t=CH)
                dst = ht[:, :, k * CH:(k + 1) * CH].rearrange("p (a b) t -> p a b t", b=4)
                e.tensor_copy(dst, src).then_inc(row_free, 1)

        @block.scalar
        def _(e):
            n = [0]

            def then(ins):
                n[0] += 1
                ins.then_inc(par_done, 1)
                e.wait_ge(par_done, n[0])

            e.wait_ge(par_t, 1)
            e.wait_ge(masks, 6)
            par = c["par"]
            then(e.activation(par[:, 0, :], ps[:, 6, 0:P], ACT.Copy))
            then(e.activation(par[:, 1, 0:81], ps[:, 6, P:P + 81], ACT.Copy))
            then(e.activation(par[:, 2, :], ps[:, 6, 2 * P:3 * P], ACT.Copy))
            e.activation(c["rg_half_gateb"][:, :], par[:, 0, A_GATEB:A_GATEB + 64], ACT.Copy, scale=0.5)
            e.activation(c["half_dn_norm"][:, :], par[:, 1, B_DNNORM:B_DNNORM + 1], ACT.Copy, scale=0.5)

    with Phase(nc) as s:
        tmp = sb(s, "sp_tmp", [P, 4, 32])
        work = sb(s, "sp_work", [P, 4, 32])
        sem = lambda n: s.semaphore(n)
        act_done, dve_done = sem("sp_act"), sem("sp_dve")
        block = s.block()
        lam = c["par"][:, 1, B_LAM:B_LAM + 32]

        @block.scalar
        def _(e):
            e.activation(tmp[:, 0, :], lam, ACT.Abs).then_inc(act_done, 1)
            e.wait_ge(act_done, 1)
            e.activation(tmp[:, 1, :], tmp[:, 0, :], ACT.Exp, scale=-1.0).then_inc(act_done, 1)
            e.activation(tmp[:, 2, :], lam, ACT.Relu, scale=-1.0).then_inc(act_done, 1)

        @block.vector
        def _(e):
            e.wait_ge(act_done, 3)
            n = softplus(e, work, tmp[:, 1, :], tmp[:, 2, :], lambda k: work[:, k, :], dve_done)
            e.tensor_scalar(c["rg_half_c"][:, :], work[:, 3, :], -4.0, None, ALU.mult)
            e.tensor_scalar(c["rg_neg_half_c"][:, :], work[:, 3, :], 4.0, None, ALU.mult) \
                .then_inc(dve_done, 1)
            e.wait_ge(dve_done, n + 1)


def softplus(e, work, expo, relu, at, done):
    n = [0]

    def then(ins):
        n[0] += 1
        ins.then_inc(done, 1)
        e.wait_ge(done, n[0])

    z, z2, p = at(0), at(1), at(2)
    then(e.tensor_scalar(z2, expo, 2.0, None, ALU.add))
    then(e.reciprocal(p, z2))
    then(e.tensor_tensor(z, expo, p, ALU.mult))
    then(e.tensor_tensor(z2, z, z, ALU.mult))
    then(e.tensor_scalar(p, z2, 1.0 / 15, None, ALU.mult))
    for k in (13, 11, 9, 7, 5, 3):
        then(e.scalar_tensor_tensor(p, p, 1.0 / k, z2, ALU.add, ALU.mult))
    then(e.scalar_tensor_tensor(p, p, 1.0, z, ALU.add, ALU.mult))
    then(e.scalar_tensor_tensor(at(3), p, 2.0, relu, ALU.mult, ALU.add))
    return n[0]


def norms(nc, sb, ps, c, tag, h_dram, y_dram, post, pre, yhi, ylo, out=None):
    par = c["par"]
    with Phase(nc) as s:
        ht = sb(s, tag + "_h", [P, KT, T])
        yt = sb(s, tag + "_y", [P, KT, T]) if y_dram is not None else None
        sq = sb(s, tag + "_sq", [P, 2, T])
        rn = sb(s, tag + "_rn", [P, 2, T])
        tmp = sb(s, tag + "_tmp", [P, 2, T])
        orow = sb(s, tag + "_orow", [CH, 2, D])
        sem = lambda n: s.semaphore(tag + n)
        h_in = [sem(f"h_in{k}") for k in range(KT)]
        y_in = [sem(f"y_in{k}") for k in range(KT)]
        squared, summed, ln_done, rn_done = sem("squared"), sem("summed"), sem("ln"), sem("rn")
        added, scaled, stored, hi_done, lo_done = (sem("added"), sem("scaled"), sem("stored"),
                                                   sem("hi"), sem("lo"))
        term = sem("term")
        turned, row_done, out_done = sem("turned"), sem("row_done"), [sem("out0"), sem("out1")]
        block = s.block()
        rounds = ([yt] if yt is not None else []) + ([ht] if pre is not None else [])

        @block.sync
        def _(e):
            for k in range(KT):
                if yt is not None:
                    e.dma_start(yt[:, k, :], y_dram[k]).then_inc(y_in[k], 16)
                e.dma_start(ht[:, k, :], h_dram[k]).then_inc(h_in[k], 16)
            if pre is not None and yt is not None:
                for k in range(KT):
                    e.wait_ge(added, k + 1)
                    e.dma_start(h_dram[k], ht[:, k, :]).then_inc(stored, 16)
                e.wait_ge(stored, 16 * KT)
            if out is not None:
                for k in range(NC):
                    e.wait_ge(row_done, k + 1)
                    if k == 0:
                        e.dma_start(out[0, 0:CH - META, :], orow[META:CH, 0, :]).then_inc(out_done[0], 16)
                    else:
                        e.dma_start(out[0, k * CH - META:(k + 1) * CH - META, :], orow[:, k % 2, :]) \
                            .then_inc(out_done[k % 2], 16)
                for b in (0, 1):
                    e.wait_ge(out_done[b], 16 * NC // 2)

        @block.scalar
        def _(e):
            for r, src in enumerate(rounds):
                for k in range(KT):
                    q = r * KT + k
                    if src is yt:
                        e.wait_ge(y_in[k], 16)
                    elif yt is None:
                        e.wait_ge(h_in[k], 16)
                    else:
                        e.wait_ge(added, k + 1)
                    if q >= 2:
                        e.wait_ge(summed, q - 1)
                    e.activation(sq[:, q % 2, :], src[:, k, :], ACT.Square).then_inc(squared, 1)
                e.wait_ge(summed, (r + 1) * KT)
                for i, (t0, tn) in enumerate(PIECES):
                    e.activation(rn[:, r, t0:t0 + tn], ps[:, 3 * r + i, 0:tn], ACT.Sqrt,
                                 scale=1.0 / D, bias=c["eps"][:, 0:1]).then_inc(ln_done, 1)
                if src is ht:
                    for k in range(KT):
                        e.wait_ge(scaled, k + 1)
                        e.activation(yhi[:, k, :], tmp[:, k % 2, :], ACT.Copy).then_inc(hi_done, 1)

        @block.tensor
        def _(e):
            for r in range(len(rounds)):
                for k in range(KT):
                    e.wait_ge(squared, r * KT + k + 1)
                    for i, (t0, tn) in enumerate(PIECES):
                        ins = e.matmul(ps[:, 3 * r + i, 0:tn], c["ones"][:, :],
                                       sq[:, (r * KT + k) % 2, t0:t0 + tn],
                                       start=(k == 0), stop=(k == KT - 1))
                    ins.then_inc(summed, 1)
            if out is not None:
                for k in range(NC):
                    e.wait_ge(added, KT)
                    if k >= 2:
                        e.wait_ge(row_done, k - 1)
                    for b in range(KT):
                        ins = e.transpose(ps[0:CH, 4 + 2 * (k % 2) + b // 4, (b % 4) * P:(b % 4 + 1) * P],
                                          ht[:, b, k * CH:(k + 1) * CH], c["ident"][:, :])
                    ins.then_inc(turned, 1)

        @block.vector
        def _(e):
            for r, src in enumerate(rounds):
                e.wait_ge(ln_done, 3 * (r + 1))
                e.reciprocal(rn[:, r, :], rn[:, r, :]).then_inc(rn_done, 1)
                e.wait_ge(rn_done, r + 1)
                w = lambda j, k: par[:, 1, B_NORM + j * KT + k:B_NORM + j * KT + k + 1]
                if src is yt:
                    for k in range(KT):
                        e.scalar_tensor_tensor(yt[:, k, :], yt[:, k, :], w(post, k), rn[:, r, :],
                                               ALU.mult, ALU.mult).then_inc(term, 1)
                        e.wait_ge(term, k + 1)
                        e.wait_ge(h_in[k], 16)
                        e.tensor_tensor(ht[:, k, :], ht[:, k, :], yt[:, k, :], ALU.add).then_inc(added, 1)
                else:
                    for k in range(KT):
                        if k >= 2:
                            e.wait_ge(hi_done, k - 1)
                            e.wait_ge(lo_done, k - 1)
                        if yt is None:
                            e.wait_ge(h_in[k], 16)
                        e.scalar_tensor_tensor(tmp[:, k % 2, :], ht[:, k, :], w(pre, k), rn[:, r, :],
                                               ALU.mult, ALU.mult).then_inc(scaled, 1)
            if out is not None:
                for k in range(NC):
                    e.wait_ge(turned, k + 1)
                    if k >= 2:
                        e.wait_ge(out_done[k % 2], 16 * (k // 2))
                    e.tensor_copy(orow[:, k % 2, :].rearrange("p (a n) -> p a n", a=2),
                                  ps[0:CH, 4 + 2 * (k % 2):6 + 2 * (k % 2), :]).then_inc(row_done, 1)

        @block.gpsimd
        def _(e):
            if pre is not None:
                for k in range(KT):
                    e.wait_ge(hi_done, k + 1)
                    e.tensor_tensor(ylo[:, k, :], tmp[:, k % 2, :], yhi[:, k, :], ALU.subtract) \
                        .then_inc(lo_done, 1)


def hold(e, passed):
    e.sem_inc(passed, 1)


class Weights:

    def __init__(self, nc, sb, s, tag, parts):
        per = len(parts)
        self.passed = s.passed
        self.parts = parts
        self.raw = sb(s, tag + "_raw", [P, 2, UNIT])
        self.hi = sb(s, tag + "_whi", [P, 2, UNIT], F32R)
        self.lo = sb(s, tag + "_wlo", [P, 2, UNIT], F32R)
        self.loaded = [s.counter(f"{tag}_w_loaded{b}", 16 * sum(parts[b::2]), 16) for b in (0, 1)]
        self.hi_done = s.counter(tag + "_w_hi", per)
        self.split = s.counter(tag + "_w_split", per, 2)

    def load(self, e, n, j, *pairs):
        e.wait_ge(self.split.sem, self.split.at(n, j - 1))
        hold(e, self.passed)
        for view, src in pairs:
            e.dma_start(view(self.raw[:, j % 2, :]), src).then_inc(self.loaded[j % 2].sem, 16)

    def split_unit(self, e, n, j, tile, used):
        slot = j % 2
        e.wait_ge(self.loaded[slot].sem, self.loaded[slot].at(n, 16 * sum(self.parts[slot:j + 1:2])))
        e.wait_ge(tile.sem, tile.at(n, used))
        hold(e, self.passed)
        e.tensor_copy(self.hi[:, slot, :], self.raw[:, slot, :]).then_inc(self.hi_done.sem, 1)
        e.wait_ge(self.hi_done.sem, self.hi_done.at(n, j + 1))
        e.tensor_tensor(self.lo[:, slot, :], self.raw[:, slot, :], self.hi[:, slot, :], ALU.subtract) \
            .then_inc(self.split.sem, 1)


def project(e, ps, bank, wt, blocks, moving, first=True, last=True):
    end = len(blocks) - 1
    for k, ((slot, col), (mhi, mlo)) in enumerate(zip(blocks, moving)):
        whi, wlo = wt.hi[:, slot, col:col + P], wt.lo[:, slot, col:col + P]
        for i, (t0, tn) in enumerate(PIECES):
            o = ps[:, bank + i, 0:tn]
            e.matmul(o, whi, mhi[:, t0:t0 + tn], start=(first and k == 0), stop=False)
            e.matmul(o, whi, mlo[:, t0:t0 + tn], start=False, stop=False)
            ins = e.matmul(o, wlo, mhi[:, t0:t0 + tn], start=False, stop=(last and k == end))
    return ins


def halves(ps, bank, row):
    yield ps[:, bank:bank + 2, 0:416], row[:, 0:832].rearrange("p (a t) -> p a t", a=2)
    yield ps[:, bank + 2, 0:208], row[:, 832:T]


def conv_taps(e, acc, xpad, weight, sem, n, base):
    for j in (1, 2, 3):
        e.scalar_tensor_tensor(acc, xpad[:, j:j + T], weight(j), acc, ALU.mult, ALU.add) \
            .then_inc(sem.sem, 1)
        e.wait_ge(sem.sem, sem.at(n, base + j))


def rg_loop(nc, sb, ps, c, yhi, ylo, w_in, gate_w, o_dram):
    with Phase(nc) as s:
        wt = Weights(nc, sb, s, "rg", (1, 1, 1, 1, 2, 2))
        xpad, xc = sb(s, "xpad", [P, 2, T + 4]), sb(s, "xc", [P, 2, T])
        xhi, xlo = sb(s, "xhi", [P, 2, T], F32R), sb(s, "xlo", [P, 2, T], F32R)
        zs = sb(s, "zs", [P, 2, T])
        a = sb(s, "a", [P, 2, 2, T])
        u = sb(s, "u", [P, 2, 2, T])
        v = sb(s, "v", [P, 2, 2, T])
        asq = sb(s, "asq", [P, T])
        apar, dpar = sb(s, "apar", [P, 2, 10]), sb(s, "dpar", [P, 3, 2])
        S = lambda name, per=0, start=1: s.counter("rg_" + name, per, start)
        tile = S("tile", 12, 5)
        apar_done, dpar_done, pad_done = S("apar", 5), S("dpar", 1), S("pad")
        x_out, tap0, taps = S("x_out", 4), S("tap0", 2), S("taps", 6)
        xhi_done, xlo_done = S("xhi", 2), S("xlo", 2)
        z_tanh, z_out = S("z_tanh", 4), S("z_out", 4)
        gate_out = S("gate_out", 16, 5)
        th_done, a_done, asq_done = S("th", 4), S("a", 4), S("asq", 4)
        v_done, u_done, s_done, b_done = S("v", 4), S("u", 4), S("s", 4), S("b", 4)
        scan, osum, odone = S("scan", 4), S("osum", 2), S("odone", 2)
        o_out = [S("o_out0", 16, 16), S("o_out1", 16, 16)]
        block = s.block()
        par = c["par"]
        DT = [(d, t) for d in range(2) for t in range(2)]

        @block.sync
        def _(e):
            cols = w_in[0].rearrange("(k p) m -> p k m", p=P)

            def store(n, ahead):
                for t in range(2):
                    e.wait_ge(odone.sem, odone.at(n, t + 1 - 2 * ahead))
                    hold(e, s.passed)
                    e.dma_start(o_dram.rearrange("a p t -> p a t")[:, bass.ds((n - ahead) * 2 + t, 1), :],
                                a[:, 0, t:t + 1, :]).then_inc(o_out[t].sem, 16)

            def turn(n, first):
                for j, off in enumerate((0, P, W, W + P)):
                    wt.load(e, n, j, (lambda r: r.rearrange("p (k m) -> p k m", k=KT),
                                      cols[:, :, bass.ds(n * 256 + off, P)]))
                if not first:
                    store(n, 1)
                for d in range(2):
                    src = gate_w[0, d].rearrange("g n (t p) m -> p g (n t) m", p=P)
                    wt.load(e, n, 4 + d, *[
                        (lambda r, g=g: r.rearrange("p (g t m) -> p g t m", g=2, t=2)[:, g],
                         src[:, g, bass.ds(n * 2, 2), :]) for g in range(2)])

            turn(0, True)
            with e.Fori(1, RG_BLOCKS) as n:
                turn(n, False)
            store(RG_BLOCKS, 1)
            for t in range(2):
                e.wait_ge(o_out[t].sem, o_out[t].at(RG_BLOCKS, 0))

        @block.gpsimd
        def _(e):
            e.memset(xpad[:, :, 0:1], 0.0)
            e.memset(xpad[:, :, T + 1:T + 4], 0.0).then_inc(pad_done.sem, 1)
            with e.Fori(0, RG_BLOCKS) as n:
                for j, used in enumerate((-4, 0, 1, 2, 3)):
                    wt.split_unit(e, n, j, tile, used)
                for t in range(2):
                    e.wait_ge(xhi_done.sem, xhi_done.at(n, t + 1))
                    e.tensor_tensor(xlo[:, t, :], xc[:, t, :], xhi[:, t, :], ALU.subtract) \
                        .then_inc(xlo_done.sem, 1)
                wt.split_unit(e, n, 5, tile, 4)

        @block.tensor
        def _(e):
            rows = [(yhi[:, k, :], ylo[:, k, :]) for k in range(KT)]
            with e.Fori(0, RG_BLOCKS) as n:
                for j in range(4):
                    e.wait_ge(wt.split.sem, wt.split.at(n, j + 1))
                    if j < 2:
                        e.wait_ge(gate_out.sem, gate_out.at(n, 2 * j - 2))
                    else:
                        e.wait_ge(x_out.sem, x_out.at(n, 2 * j - 2))
                    project(e, ps, 3 * (j % 2), wt, [(j % 2, k * P) for k in range(KT)], rows) \
                        .then_inc(tile.sem, 1)
                e.wait_ge(xlo_done.sem, xlo_done.at(n, 2))
                conv = [(xhi[:, i, :], xlo[:, i, :]) for i in range(2)]
                for q in range(8):
                    d, g, t = q // 4, q // 2 % 2, q % 2
                    if q % 4 == 0:
                        e.wait_ge(wt.split.sem, wt.split.at(n, 5 + d))
                    if q < 2:
                        e.wait_ge(z_out.sem, z_out.at(n, 2 * q + 2))
                    else:
                        e.wait_ge(gate_out.sem, gate_out.at(n, 2 * q - 2))
                    project(e, ps, 3 * (q % 2), wt, [(d, g * 512 + i * 256 + t * P) for i in range(2)],
                            conv).then_inc(tile.sem, 1)

        @block.scalar
        def _(e):
            e.wait_ge(pad_done.sem, pad_done.at(0, 1))
            pick = lambda n, src, k: src.rearrange("p (a t) -> p a t", t=WT)[:, 0:k, bass.ds(n * 2, 2)] \
                .rearrange("p a t -> p t a")
            with e.Fori(0, RG_BLOCKS) as n:
                e.wait_ge(gate_out.sem, gate_out.at(n, 0))
                e.wait_ge(a_done.sem, a_done.at(n, 0))
                col = 0
                for src, k in ((par[:, 0, A_CONV:A_CONV + 16], 1), (par[:, 1, B_CONVB:B_CONVB + 16], 1),
                               (c["rg_half_c"][:, :], 2), (c["rg_neg_half_c"][:, :], 2),
                               (c["rg_half_gateb"][:, :], 4)):
                    e.activation(apar[:, :, col:col + k], pick(n, src, k), ACT.Copy) \
                        .then_inc(apar_done.sem, 1)
                    col += k
                e.wait_ge(apar_done.sem, apar_done.at(n, 5))
                ap = lambda t, k: apar[:, t, k:k + 1]
                for t in range(2):
                    e.wait_ge(tile.sem, tile.at(n, t + 1))
                    e.wait_ge(taps.sem, taps.at(n, 0))
                    for src, dst in halves(ps, 3 * t, xpad[:, t, 1:T + 1]):
                        e.activation(dst, src, ACT.Copy).then_inc(x_out.sem, 1)
                    e.wait_ge(x_out.sem, x_out.at(n, 2 * t + 2))
                    e.wait_ge(v_done.sem, v_done.at(n, 0))
                    e.wait_ge(xlo_done.sem, xlo_done.at(n, 0))
                    e.activation(xc[:, t, :], xpad[:, t, 0:T], ACT.Identity, scale=ap(t, 0),
                                 bias=ap(t, 1)).then_inc(tap0.sem, 1)
                for t in range(2):
                    e.wait_ge(tile.sem, tile.at(n, t + 3))
                    e.wait_ge(odone.sem, odone.at(n, 0))
                    for src, dst in halves(ps, 3 * t, zs[:, t, :]):
                        e.activation(dst, src, ACT.Tanh, scale=0.5).then_inc(z_tanh.sem, 1)
                    e.wait_ge(taps.sem, taps.at(n, 3 * t + 3))
                    e.activation(xhi[:, t, :], xc[:, t, :], ACT.Copy).then_inc(xhi_done.sem, 1)
                for d in range(2):
                    for g in range(2):
                        for t in range(2):
                            q = 4 * d + 2 * g + t
                            e.wait_ge(tile.sem, tile.at(n, q + 5))
                            if q == 0:
                                for b in range(2):
                                    e.wait_ge(o_out[b].sem, o_out[b].at(n, 0))
                                e.wait_ge(scan.sem, scan.at(n, 0))
                            dst_row = (a, v)[g][:, d, t, :]
                            for src, dst in halves(ps, 3 * t, dst_row):
                                e.activation(dst, src, ACT.Tanh, scale=0.5,
                                             bias=ap(t, 6 + 2 * d + g)).then_inc(gate_out.sem, 1)
                for i, (d, t) in enumerate(DT):
                    if i == 0:
                        e.wait_ge(gate_out.sem, gate_out.at(n, 16))
                        e.wait_ge(osum.sem, osum.at(n, 0))
                    e.activation(u[:, d, t, :], a[:, d, t, :], ACT.Tanh, scale=ap(t, 4 + d),
                                 bias=ap(t, 4 + d)).then_inc(th_done.sem, 1)
                    e.wait_ge(th_done.sem, th_done.at(n, i + 1))
                    e.activation(a[:, d, t, :], a[:, d, t, :], ACT.Exp, scale=ap(t, 2 + d),
                                 bias=ap(t, 2 + d)).then_inc(a_done.sem, 1)
                    e.wait_ge(a_done.sem, a_done.at(n, i + 1))
                    e.wait_ge(u_done.sem, u_done.at(n, i))
                    e.activation(asq[:, :], a[:, d, t, :], ACT.Square).then_inc(asq_done.sem, 1)
                for i, (d, t) in enumerate(DT):
                    e.wait_ge(u_done.sem, u_done.at(n, i + 1))
                    e.activation(u[:, d, t, :], u[:, d, t, :], ACT.Sqrt).then_inc(s_done.sem, 1)

        @block.vector
        def _(e):
            with e.Fori(0, RG_BLOCKS) as n:
                e.wait_ge(taps.sem, taps.at(n, 0))
                taps_of = par[:, 0, A_CONV:A_CONV + 64].rearrange("p (j t) -> p j t", t=WT)
                e.tensor_copy(dpar[:, :, :], taps_of[:, 1:4, bass.ds(n * 2, 2)]).then_inc(dpar_done.sem, 1)
                e.wait_ge(dpar_done.sem, dpar_done.at(n, 1))
                for t in range(2):
                    e.wait_ge(tap0.sem, tap0.at(n, t + 1))
                    conv_taps(e, xc[:, t, :], xpad[:, t, :], lambda j: dpar[:, j - 1, t:t + 1], taps, n, 3 * t)
                for t in range(2):
                    e.wait_ge(z_tanh.sem, z_tanh.at(n, 2 * t + 2))
                    for src, dst in halves(ps, 3 * t, zs[:, t, :]):
                        e.scalar_tensor_tensor(dst, dst, 1.0, src, ALU.add, ALU.mult) \
                            .then_inc(z_out.sem, 1)
                for i, (d, t) in enumerate(DT):
                    e.wait_ge(gate_out.sem, gate_out.at(n, 2 * (4 * d + 2 + t) + 2))
                    e.scalar_tensor_tensor(v[:, d, t, :], v[:, d, t, :], 1.0, xc[:, t, :],
                                           ALU.add, ALU.mult).then_inc(v_done.sem, 1)
                for i, (d, t) in enumerate(DT):
                    e.wait_ge(asq_done.sem, asq_done.at(n, i + 1))
                    e.scalar_tensor_tensor(u[:, d, t, :], asq[:, :], 1.0, u[:, d, t, :],
                                           ALU.add, ALU.mult).then_inc(u_done.sem, 1)
                for i, (d, t) in enumerate(DT):
                    e.wait_ge(s_done.sem, s_done.at(n, i + 1))
                    e.wait_ge(v_done.sem, v_done.at(n, i + 1))
                    e.scalar_tensor_tensor(v[:, d, t, :], u[:, d, t, :], 0.5, v[:, d, t, :],
                                           ALU.mult, ALU.mult).then_inc(b_done.sem, 1)
                    e.wait_ge(b_done.sem, b_done.at(n, i + 1))
                    order = slice(None) if d == 0 else slice(None, None, -1)
                    states = a[:, 0, t, :] if d == 0 else u[:, 1, t, :]
                    e.tensor_tensor_scan(states[:, order], a[:, d, t, order], v[:, d, t, order], 0.0,
                                         ALU.mult, ALU.add).then_inc(scan.sem, 1)
                for t in range(2):
                    e.wait_ge(scan.sem, scan.at(n, 3 + t))
                    e.tensor_tensor(a[:, 0, t, :], a[:, 0, t, :], u[:, 1, t, :], ALU.add) \
                        .then_inc(osum.sem, 1)
                for t in range(2):
                    e.wait_ge(osum.sem, osum.at(n, t + 1))
                    e.scalar_tensor_tensor(a[:, 0, t, :], a[:, 0, t, :], 0.5, zs[:, t, :],
                                           ALU.mult, ALU.mult).then_inc(odone.sem, 1)


def out_projection(nc, sb, ps, tag, w_out, o_dram, y_dram):
    with Phase(nc) as s:
        ohi, olo = sb(s, tag + "_ohi", [P, WT, T], F32R), sb(s, tag + "_olo", [P, WT, T], F32R)
        oraw = sb(s, tag + "_oraw", [P, 2, T])
        wt = Weights(nc, sb, s, tag, (1, 1, 1, 1))
        yo = sb(s, tag + "_yo", [P, 2, T])
        S = lambda name, per=0, start=1: s.counter(tag + "_" + name, per, start)
        o_in = [S("o_in0", 0, 16), S("o_in1", 0, 16)]
        hi_done, lo_done = S("ohi"), S("olo")
        step = S("step", 4, 2)
        y_out = S("y_out", 4)
        stored = [S("stored0", 16, 16), S("stored1", 16, 16)]
        block = s.block()
        OPU = 4

        @block.sync
        def _(e):
            src = w_out[0].rearrange("(u k p) m -> p u k m", p=P, k=OPU)
            with e.Fori(0, KT // 2) as n:
                for j in range(4):
                    wt.load(e, n, j, (lambda r: r.rearrange("p (k m) -> p k m", k=OPU),
                                      src[:, j, :, bass.ds(n * 2 * P, 2 * P)]))
                for t in range(2):
                    e.wait_ge(y_out.sem, y_out.at(n, 2 * t + 2))
                    hold(e, s.passed)
                    e.dma_start(y_dram.rearrange("a p t -> p a t")[:, bass.ds(n * 2 + t, 1), :],
                                yo[:, t:t + 1, :]).then_inc(stored[t].sem, 16)
            for t in range(2):
                e.wait_ge(stored[t].sem, stored[t].at(KT // 2, 0))

        @block.scalar
        def _(e):
            for k in range(WT):
                if k >= 2:
                    e.wait_ge(lo_done.sem, lo_done.at(0, k - 1))
                e.dma_start(oraw[:, k % 2, :], o_dram[k]).then_inc(o_in[k % 2].sem, 16)
                if k >= 1:
                    e.wait_ge(o_in[(k - 1) % 2].sem, o_in[0].at(0, 16 * ((k - 1) // 2 + 1)))
                    e.activation(ohi[:, k - 1, :], oraw[:, (k - 1) % 2, :], ACT.Copy) \
                        .then_inc(hi_done.sem, 1)
            e.wait_ge(o_in[1].sem, o_in[1].at(0, 16 * WT // 2))
            e.activation(ohi[:, WT - 1, :], oraw[:, 1, :], ACT.Copy).then_inc(hi_done.sem, 1)
            with e.Fori(0, KT // 2) as n:
                for t in range(2):
                    e.wait_ge(step.sem, step.at(n, 4))
                    e.wait_ge(stored[t].sem, stored[t].at(n, 0))
                    for src, dst in halves(ps, 3 * t, yo[:, t, :]):
                        e.activation(dst, src, ACT.Copy).then_inc(y_out.sem, 1)

        @block.vector
        def _(e):
            for k in range(WT):
                e.wait_ge(hi_done.sem, hi_done.at(0, k + 1))
                e.tensor_tensor(olo[:, k, :], oraw[:, k % 2, :], ohi[:, k, :], ALU.subtract) \
                    .then_inc(lo_done.sem, 1)

        @block.gpsimd
        def _(e):
            with e.Fori(0, KT // 2) as n:
                for j in range(4):
                    wt.split_unit(e, n, j, step, j - 1)

        @block.tensor
        def _(e):
            def turn(n, first):
                e.wait_ge(y_out.sem, y_out.at(n, 0))
                for j in range(4):
                    e.wait_ge(wt.split.sem, wt.split.at(n, j + 1))
                    for i in range(OPU):
                        k = OPU * j + i
                        if first:
                            e.wait_ge(lo_done.sem, lo_done.at(0, k + 1))
                        for t in range(2):
                            ins = project(e, ps, 3 * t, wt, [(j % 2, i * 2 * P + t * P)],
                                          [(ohi[:, k, :], olo[:, k, :])], k == 0, k == WT - 1)
                    ins.then_inc(step.sem, 1)
            turn(0, True)
            with e.Fori(1, KT // 2) as n:
                turn(n, False)


def dn_tables(nc, sb, ps, c, t, yhi, ylo, w_in, a_log, dt_bias, rows_dram):
    AB = 4 * V_HEADS
    HD = 2 * V_HEADS
    off = 3 * W
    with Phase(nc) as s:
        wraw = sb(s, "ab_raw", [P, KT, AB])
        whi, wlo = sb(s, "ab_hi", [P, KT, AB], F32R), sb(s, "ab_lo", [P, KT, AB], F32R)
        consts = sb(s, "ab_consts", [CH, 3, HD])
        xa, ex, rl = sb(s, "ab_x", [CH, NC, HD]), sb(s, "ab_ex", [CH, NC, HD]), sb(s, "ab_rl", [CH, NC, HD])
        work = sb(s, "ab_work", [CH, 4, NC * HD])
        btok, eg_tok = sb(s, "ab_beta", [CH, NC, HD]), sb(s, "ab_eg", [CH, NC, HD])
        rows = sb(s, "ab_rows", [HD, 2, T])
        sem = lambda n: s.semaphore("ab_" + n)
        w_load, c_load, w_hi, w_lo, ab, act, dve = (sem(n) for n in
                                                   ("w_load", "c_load", "w_hi", "w_lo", "ab", "act", "dve"))
        sp, sums, tabs, row_t, row_out, stored, gdone = (sem(n) for n in
                                                        ("sp", "sums", "tabs", "row_t", "row_out", "stored", "g"))
        block = s.block()

        @block.sync
        def _(e):
            e.dma_start(wraw[:, :, :], w_in[0].rearrange("(k p) m -> p k m", p=P)[:, :, off:off + AB]) \
                .then_inc(w_load, 16)
            for i, src in enumerate((dt_bias, a_log)):
                e.dma_start(consts[:, i, :], src.rearrange("a d h -> (a d h)").partition_broadcast(CH)) \
                    .then_inc(c_load, 16)
            for i in range(2):
                e.wait_ge(row_out, 3 * (i + 1))
                e.dma_start(rows_dram[i], rows[:, i, :]).then_inc(stored, 16)
            e.wait_ge(stored, 32)

        @block.gpsimd
        def _(e):
            e.wait_ge(w_load, 16)
            e.tensor_copy(whi[:, :, :], wraw[:, :, :]).then_inc(w_hi, 1)
            e.wait_ge(w_hi, 1)
            e.tensor_tensor(wlo[:, :, :], wraw[:, :, :], whi[:, :, :], ALU.subtract).then_inc(w_lo, 1)

        @block.tensor
        def _(e):
            e.wait_ge(w_lo, 1)
            for k in range(NC):
                o = ps[0:CH, k // 8, (k % 8) * AB:(k % 8 + 1) * AB]
                for i in range(KT):
                    yh, yl = (y[:, i, k * CH:(k + 1) * CH] for y in (yhi, ylo))
                    e.matmul(o, yh, whi[:, i, :], start=(i == 0), stop=False)
                    e.matmul(o, yh, wlo[:, i, :], start=False, stop=False)
                    ins = e.matmul(o, yl, whi[:, i, :], start=False, stop=(i == KT - 1))
            ins.then_inc(ab, 1)
            e.wait_ge(gdone, 1)
            for d in range(2):
                g = t["g"][:, d, :, :]
                cols = slice(d * NC * V_HEADS, (d + 1) * NC * V_HEADS)
                e.matmul(ps[0:CH, 2, cols], c["upto"][:, d, :], g, start=True, stop=True)
                e.matmul(ps[0:CH, 3, cols], c["after"][:, d, :], g, start=True, stop=True)
                ins = e.matmul(ps[:, 4, cols], c["ones"][0:CH, :], g, start=True, stop=True)
            ins.then_inc(sums, 1)
            for i in range(2):
                if i == 0:
                    e.wait_ge(tabs, 3)
                else:
                    e.wait_ge(row_out, 3)
                for k in range(NC):
                    src = eg_tok[:, k, :] if i == 0 else btok[:, k, :]
                    ins = e.transpose(ps[0:HD, 5 + k // CPB, (k % CPB) * CH:(k % CPB + 1) * CH], src,
                                      c["ident"][0:CH, 0:CH])
                ins.then_inc(row_t, 1)

        @block.scalar
        def _(e):
            e.wait_ge(dve, 2)
            for k0, k1 in ((0, 8), (8, NC)):
                src = ps[0:CH, k0 // 8, 0:(k1 - k0) * AB].rearrange("p (k m) -> p k m", m=AB)
                e.activation(btok[:, k0:k1, :], src[:, :, HD:AB], ACT.Tanh, scale=0.5).then_inc(act, 1)
            e.activation(ex[:, :, :], xa[:, :, :], ACT.Abs).then_inc(act, 1)
            e.wait_ge(act, 3)
            e.activation(ex[:, :, :], ex[:, :, :], ACT.Exp, scale=-1.0).then_inc(act, 1)
            e.activation(rl[:, :, :], xa[:, :, :], ACT.Relu).then_inc(act, 1)
            e.wait_ge(c_load, 32)
            e.activation(consts[:, 2, :], consts[:, 1, :], ACT.Exp).then_inc(act, 1)
            e.wait_ge(sums, 1)
            for i, name in enumerate(("eg", "tail", "gt")):
                rows_ = P if name == "gt" else CH
                src = ps[0:rows_, 2 + i, 0:NC * HD].rearrange("p (d k h) -> p d k h", d=2, k=NC)
                e.activation(t[name][:, :, :, :], src, ACT.Exp).then_inc(tabs, 1)
                if i == 0:
                    for d in range(2):
                        order = slice(None) if d == 0 else slice(None, None, -1)
                        e.activation(eg_tok[:, order, d * V_HEADS:(d + 1) * V_HEADS], src[:, d],
                                     ACT.Exp).then_inc(tabs, 1)
            for i in range(2):
                e.wait_ge(row_t, i + 1)
                for b, (t0, tn) in enumerate(PIECES):
                    e.activation(rows[:, i, t0:t0 + tn], ps[0:HD, 5 + b, 0:tn], ACT.Copy).then_inc(row_out, 1)

        @block.vector
        def _(e):
            e.wait_ge(ab, 1)
            e.wait_ge(c_load, 32)
            for k0, k1 in ((0, 8), (8, NC)):
                src = ps[0:CH, k0 // 8, 0:(k1 - k0) * AB].rearrange("p (k m) -> p k m", m=AB)
                e.tensor_tensor(xa[:, k0:k1, :], src[:, :, 0:HD],
                                consts[:, 0, :].unsqueeze(1).to_broadcast([CH, k1 - k0, HD]), ALU.add) \
                    .then_inc(dve, 1)
            e.wait_ge(act, 6)
            flat = lambda v: v[:, :, :].rearrange("p k m -> p (k m)")
            softplus(e, work, flat(ex), flat(rl), lambda k: work[:, k, :], sp)
            for d in range(2):
                order = slice(None) if d == 0 else slice(None, None, -1)
                hd = slice(d * V_HEADS, (d + 1) * V_HEADS)
                spv = work[:, 3, :].rearrange("p (k m) -> p k m", m=HD)[:, order, hd]
                ea = consts[:, 2, hd].unsqueeze(1).to_broadcast([CH, NC, V_HEADS])
                e.scalar_tensor_tensor(t["g"][:, d, :, :], spv, -1.0, ea, ALU.mult, ALU.mult) \
                    .then_inc(dve, 1)
            e.wait_ge(dve, 4)
            e.tensor_scalar(btok[:, :, :], btok[:, :, :], 0.5, 0.5, ALU.mult, ALU.add).then_inc(gdone, 1)
            e.wait_ge(gdone, 1)
            for d in range(2):
                order = slice(None) if d == 0 else slice(None, None, -1)
                e.tensor_copy(t["beta"][:, d, :, :], btok[:, order, d * V_HEADS:(d + 1) * V_HEADS]) \
                    .then_inc(dve, 1)
            e.wait_ge(dve, 6)


def dn_loop(nc, sb, ps, c, tabs, yhi, ylo, w_in, rows_dram, o_dram):
    PAIRS = NC // 2
    VO = 4 * P
    with Phase(nc) as s:
        wt = Weights(nc, sb, s, "dn", (1,) * 6)
        qk = sb(s, "qk", [P, 2, T])
        vo = sb(s, "vo", [P, 2, T])
        vrow, krow = sb(s, "vrow", [CH, NC, 2, P]), sb(s, "krow", [CH, NC, P])
        zs = sb(s, "dzs", [P, 2, T])
        m4 = 4 * CH
        work = sb(s, "dn_work", [P, 24 * m4 + 6 * VO])
        whi, wlo = (v[0:CH, :, :].rearrange("p a b -> p (a b)") for v in (wt.hi, wt.lo))
        shape = dict(m=4, i=CH)
        nhr = whi[:, 0:4 * m4].rearrange("p (b m i) -> p b m i", **shape)
        xx = wlo[:, 0:2 * m4].rearrange("p (b m i) -> p b m i", **shape)
        xt = wlo[:, 2 * m4:4 * m4].rearrange("p (b m i) -> p b m i", **shape)
        xt1, pp = (sb(s, k, [CH, 2, 4, CH], F32R) for k in ("xt1", "pp"))
        used = [0]

        def part(rows, *shape):
            size = int(np.prod(shape))
            v = work[0:rows, used[0]:used[0] + size]
            used[0] += size
            names = "abcde"[:len(shape)]
            if len(shape) == 1:
                return v
            return v.rearrange(f"p ({' '.join(names)}) -> p {' '.join(names)}",
                               **{n: k for n, k in zip(names, shape)})

        xpad, tht = part(P, 2, T + 4), part(P, 2, T)
        sq, rn = part(P, 2, T), part(P, 2, T)
        used[0] = 0
        gm = part(CH, 2, 2, 2, CH)
        ee, lg, tb = (part(CH, 2, 4, CH) for _ in range(3))
        nh, qkt = part(CH, 4, 4, CH), part(CH, 4, 4, CH)
        qd, bring = part(P, 2, 4, CH), part(CH, 2, 4, CH)
        kt, st = part(CH, 2, 4, P), part(P, 2, 4, P)
        rr, vn = part(CH, 4, P), part(CH, 4, P)
        head = {k: sb(s, "head_" + k, [P if k == "gt" else CH, 2, NC, 2]) for k in ("g", "eg", "tail", "gt", "beta")}
        dpar = sb(s, "dn_dpar", [P, 4, 4])
        S = lambda name, per=0, start=1: s.counter("dn_" + name, per, start)
        tile = S("tile", 6, 2)
        pad_done, heads = S("pad", 1), S("heads", 5)
        ident_r, eye_done = sb(s, "ident_r", [CH, 2, CH], F32R), S("eye")
        x_out, tap0, taps, th_done, silu = S("x_out", 8), S("tap0", 4), S("taps", 12), S("th", 4), S("silu", 4)
        z_tanh, z_out = S("z_tanh", 4), S("z_out", 4)
        sq_done, ssum, ln_done, rn_done, normed = S("sq", 4), S("ssum", 4), S("ln", 8), S("rn", 4), S("normed", 2)
        turned, row_done = S("turned", 8), S("row_done", 8)
        b_in, c_in = [S(f"b_in{i}", 32 * PAIRS, 16) for i in (0, 1)], [S(f"c_in{i}", 32 * PAIRS, 16) for i in (0, 1)]
        lg_done, gram, dmat, gm_done, e_done = S("lg", NC), S("gram", NC), S("dmat", NC), S("gm", NC), S("e", NC)
        nb_done, nt_done, x1t_done, qkt_done = S("nb", NC), S("nt", 2 * NC), S("x1t", NC), S("qkt", NC)
        pm, pev = S("pm", (LEVELS + 1) * NC), S("pev", (LEVELS + 1) * NC)
        xm, xev = S("xm", 6 * NC), S("xev", 6 * NC)
        xtm, tb_done = S("xtm", 7 * NC), S("tb", NC)
        xtev = [S(f"xtev{b}", 6 * PAIRS) for b in (0, 1)]
        qd_done, kt_done, s_init = S("qd", NC), S("kt", NC), S("s_init", 1)
        ksm, r_done, vm, vn_done = S("ksm", NC), S("r", NC), S("vm", NC), S("vn", NC)
        om, sm, oacc, snew = S("om", NC), S("sm", NC), S("oacc", 2 * NC), S("snew", NC)
        scaled, gated = S("scaled", 2), S("gated", 2)
        o_out = [S("o_out0", 16, 16), S("o_out1", 16, 16)]
        block = s.block()
        par = c["par"]
        chunk = lambda st_, d: (st_ if d == 0 else NC - 1 - st_)
        cs = lambda st_, d: slice(chunk(st_, d) * CH, (chunk(st_, d) + 1) * CH)
        D4 = lambda v: v.rearrange("p (d r) i -> p d r i", d=2)
        OFF = (W // 2, 0, W, W + P, 2 * W, 2 * W + P)
        MUL = (P, P, 2 * P, 2 * P, 2 * P, 2 * P)
        dsts = (qk[:, 0, :], qk[:, 1, :], vo[:, 0, :], vo[:, 1, :])

        def nth(st_, i, k):
            return st_ // 2 * 2 * k + 2 * i + st_ % 2 + 1

        def schedule(e, n, pre, first, level, state):
            for p in range(-1, PAIRS + 1):
                for l in range(LEVELS + 1):
                    if 0 <= p < PAIRS:
                        for st_ in (2 * p, 2 * p + 1):
                            first(st_, l)
                    if p + 1 < PAIRS:
                        for st_ in (2 * p + 2, 2 * p + 3):
                            pre(st_, l)
                    if p >= 1 and l < 6:
                        state(2 * p - 2 + l // 3, l % 3)
                    if 0 <= p < PAIRS:
                        for st_ in (2 * p, 2 * p + 1):
                            level(st_, l)

        @block.sync
        def _(e):
            cols = w_in[0].rearrange("(k p) m -> p k m", p=P)
            rows = [rows_dram[i].rearrange("(d h) t -> d h t", d=2) for i in range(2)]

            def load(n, j):
                wt.load(e, n, j, (lambda r: r.rearrange("p (k m) -> p k m", k=KT),
                                  cols[:, :, bass.ds(n * MUL[j] + OFF[j], P)]))

            def rows_of(n, i, ring, sems, free, per, st_):
                b = st_ % 2
                if st_ < 2:
                    e.wait_ge(normed.sem, normed.at(n, 2))
                else:
                    e.wait_ge(free.sem, free.at(n, per * (st_ - 1)))
                hold(e, s.passed)
                for d in range(2):
                    src = rows[i][d][bass.ds(n * 2, 2), cs(st_, d)]
                    e.dma_start(ring[:, b, 2 * d:2 * d + 2, :],
                                src.partition_broadcast(P if i == 0 else CH)).then_inc(sems[b].sem, 16)

            def turn(n, last):
                for j in range(2, 6):
                    load(n, j)
                for st_ in (0, 1):
                    rows_of(n, 1, bring, b_in, nt_done, 2, st_)
                for p in range(PAIRS):
                    for st_ in (2 * p, 2 * p + 1):
                        rows_of(n, 0, qd, c_in, om, 1, st_)
                    if p + 1 < PAIRS:
                        for st_ in (2 * p + 2, 2 * p + 3):
                            rows_of(n, 1, bring, b_in, nt_done, 2, st_)
                if not last:
                    load(n + 1, 0), load(n + 1, 1)
                for r in range(2):
                    e.wait_ge(gated.sem, gated.at(n, r + 1))
                    hold(e, s.passed)
                    e.dma_start(o_dram.rearrange("a p t -> p a t")[:, bass.ds(n * 2 + r, 1), :],
                                vo[:, r:r + 1, :]).then_inc(o_out[r].sem, 16)

            load(0, 0), load(0, 1)
            with e.Fori(0, QK_HEADS - 1) as n:
                turn(n, False)
            turn(QK_HEADS - 1, True)
            for r in range(2):
                e.wait_ge(o_out[r].sem, o_out[r].at(QK_HEADS, 0))

        @block.gpsimd
        def _(e):
            e.tensor_copy(ident_r[:, 0, :], c["ident"][0:CH, 0:CH])
            e.tensor_scalar(ident_r[:, 1, :], c["ident"][0:CH, 0:CH], -1.0, None, ALU.mult).then_inc(eye_done.sem, 1)
            with e.Fori(0, QK_HEADS) as n:
                e.wait_ge(gated.sem, gated.at(n, 0))
                hold(e, s.passed)
                e.memset(xpad[:, :, 0:1], 0.0)
                e.memset(xpad[:, :, T + 1:T + 4], 0.0).then_inc(pad_done.sem, 1)
                for j in range(6):
                    wt.split_unit(e, n, j, tile, j - 1)
                e.wait_ge(normed.sem, normed.at(n, 2))
                e.wait_ge(heads.sem, heads.at(n, 5))
                hold(e, s.passed)
                e.memset(st[:, 0, :, :], 0.0).then_inc(s_init.sem, 1)

                eye = c["ident"][0:CH, 0:CH].unsqueeze(1).to_broadcast([CH, 4, CH])

                def pre(st_, l):
                    b, q4 = st_ % 2, st_ % 4
                    if l == 0:
                        if st_ >= 2:
                            e.wait_ge(dmat.sem, dmat.at(n, st_ - 1))
                        e.tensor_tensor(D4(lg[:, b, :, :]),
                                        c["after"][:, :, :].unsqueeze(2).to_broadcast([CH, 2, 2, CH]),
                                        head["g"][:, :, st_, :].unsqueeze(3).to_broadcast([CH, 2, 2, CH]),
                                        ALU.mult).then_inc(lg_done.sem, 1)
                    if l != 5:
                        return
                    e.wait_ge(nb_done.sem, nb_done.at(n, st_ + 1))
                    e.wait_ge(b_in[b].sem, b_in[b].at(n, 32 * (st_ // 2 + 1)))
                    e.tensor_tensor(nh[:, q4, :, :], nh[:, q4, :, :], bring[:, b, :, :], ALU.mult) \
                        .then_inc(nt_done.sem, 1)
                    e.wait_ge(nt_done.sem, nt_done.at(n, 2 * st_ + 1))
                    if st_ >= 4:
                        e.wait_ge(pm.sem, pm.at(n, nth(st_ - 4, 6, 8)))
                    e.tensor_tensor(nhr[:, q4, :, :], nh[:, q4, :, :], eye, ALU.add).then_inc(nt_done.sem, 1)
                    e.wait_ge(nt_done.sem, nt_done.at(n, 2 * st_ + 2))
                    if st_ >= 2:
                        e.wait_ge(xtm.sem, xtm.at(n, nth(st_ - 2, 0, 7)))
                    lm0 = c["level_mask"][:, 0, :, 0:CH]
                    for d in range(2):
                        ins = e.tensor_tensor(D4(xt1[:, b, :, :])[:, d], D4(nhr[:, q4, :, :])[:, d],
                                              lm0[:, 1 - d, :].unsqueeze(1).to_broadcast([CH, 2, CH]),
                                              ALU.mult)
                    ins.then_inc(x1t_done.sem, 1)

                def state(st_, piece):
                    if piece != 0:
                        return
                    b = st_ % 2
                    e.wait_ge(c_in[b].sem, c_in[b].at(n, 32 * (st_ // 2 + 1)))
                    if st_ >= 2:
                        e.wait_ge(sm.sem, sm.at(n, st_ - 1))
                    for d in range(2):
                        ins = e.tensor_tensor(qd[:, b, 2 * d:2 * d + 2, :], qd[:, b, 2 * d:2 * d + 2, :],
                                              qk[:, 1, cs(st_, d)].unsqueeze(1).to_broadcast([P, 2, CH]),
                                              ALU.mult)
                    ins.then_inc(qd_done.sem, 1)
                    for d in range(2):
                        ins = e.tensor_tensor(kt[:, b, 2 * d:2 * d + 2, :],
                                              krow[:, chunk(st_, d), :].unsqueeze(1).to_broadcast([CH, 2, P]),
                                              head["tail"][:, d, st_, :].unsqueeze(2).to_broadcast([CH, 2, P]),
                                              ALU.mult)
                    ins.then_inc(kt_done.sem, 1)

                schedule(e, n, pre, lambda *_: None, lambda *_: None, state)

        @block.tensor
        def _(e):
            moving = [(yhi[:, k, :], ylo[:, k, :]) for k in range(KT)]
            e.wait_ge(eye_done.sem, eye_done.at(0, 1))
            with e.Fori(0, QK_HEADS) as n:
                for j in range(6):
                    e.wait_ge(wt.split.sem, wt.split.at(n, j + 1))
                    if j < 2:
                        e.wait_ge(ln_done.sem, ln_done.at(n, 0))
                    elif j < 6:
                        e.wait_ge(x_out.sem, x_out.at(n, 2 * j - 2))
                    project(e, ps, 3 * (j % 2), wt, [(j % 2, k * P) for k in range(KT)], moving) \
                        .then_inc(tile.sem, 1)
                for g in range(5):
                    if g == 0:
                        e.wait_ge(silu.sem, silu.at(n, 4))
                        e.wait_ge(snew.sem, snew.at(n, 0))
                    elif g >= 2:
                        e.wait_ge(row_done.sem, row_done.at(n, g - 1))
                    for i in range(4):
                        k = 2 * g + i // 2
                        ins = e.transpose(ps[0:CH, 6 + g % 2, i * P:(i + 1) * P],
                                          vo[:, i % 2, k * CH:(k + 1) * CH], c["ident"][:, :])
                    ins.then_inc(turned.sem, 1)
                for i in range(2):
                    e.wait_ge(sq_done.sem, sq_done.at(n, i + 1))
                    e.wait_ge(z_out.sem, z_out.at(n, 2 * i + 2))
                    for b, (t0, tn) in enumerate(PIECES):
                        ins = e.matmul(ps[:, 3 * i + b, 0:tn], c["ones"][:, :], sq[:, i, t0:t0 + tn],
                                       start=True, stop=True)
                    ins.then_inc(ssum.sem, 1)
                for g in range(5, 8):
                    e.wait_ge(normed.sem, normed.at(n, 1))
                    e.wait_ge(row_done.sem, row_done.at(n, g - 1))
                    for k in range(4 * (g - 5), min(4 * (g - 4), NC)):
                        ins = e.transpose(ps[0:CH, 6 + g % 2, (k % 4) * P:(k % 4 + 1) * P],
                                          qk[:, 0, k * CH:(k + 1) * CH], c["ident"][:, :])
                    ins.then_inc(turned.sem, 1)

                def pre(st_, l):
                    b = st_ % 2
                    if l == 1:
                        if st_ < 2:
                            e.wait_ge(normed.sem, normed.at(n, 2))
                        else:
                            e.wait_ge(e_done.sem, e_done.at(n, st_ - 1))
                        for d in range(2):
                            ins = e.matmul(ps[0:CH, 4 + b, d * 2 * CH:(d + 1) * 2 * CH], qk[:, 0, cs(st_, d)],
                                           qk[:, :, cs(st_, d)], start=True, stop=True)
                        ins.then_inc(gram.sem, 1)
                    elif l == 3:
                        e.wait_ge(lg_done.sem, lg_done.at(n, st_ + 1))
                        e.wait_ge(gm_done.sem, gm_done.at(n, st_ + 1))
                        for m in range(4):
                            ins = e.matmul(ps[0:CH, 4 + b, m * CH:(m + 1) * CH], lg[:, b, m, :],
                                           c["upto"][:, m // 2, :], start=True, stop=True)
                        ins.then_inc(dmat.sem, 1)

                def first(st_, l):
                    b, q4 = st_ % 2, st_ % 4
                    if l == 0:
                        e.wait_ge(nt_done.sem, nt_done.at(n, 2 * st_ + 2))
                        if st_ >= 2:
                            e.wait_ge(pev.sem, pev.at(n, nth(st_ - 2, 7, 8)))
                    elif l == 1:
                        e.wait_ge(pev.sem, pev.at(n, nth(st_, 0, 8)))
                    else:
                        e.wait_ge(xev.sem, xev.at(n, nth(st_, l - 2, 6)))
                    for m in range(4):
                        o = ps[0:CH, 2 * b, m * CH:(m + 1) * CH]
                        if l < LEVELS:
                            rhs = ident_r[:, 0, :] if l == 0 else xx[:, b, m, :]
                            ins = e.matmul(o, nhr[:, q4, m, :], rhs, start=True, stop=True)
                        else:
                            e.matmul(o, nh[:, q4, m, :], xx[:, b, m, :].bitcast(F32), start=True, stop=False)
                            ins = e.matmul(o, ident_r[:, 1, :], xx[:, b, m, :], start=False, stop=True)
                    ins.then_inc(pm.sem, 1)

                def level(st_, l):
                    b = st_ % 2
                    if l == 0:
                        return
                    xt_ = (xt1 if l == 1 else xt)[:, b]
                    e.wait_ge(pev.sem, pev.at(n, nth(st_, l, 8)))
                    if l == 1:
                        e.wait_ge(x1t_done.sem, x1t_done.at(n, st_ + 1))
                        if st_ >= 2:
                            e.wait_ge(tb_done.sem, tb_done.at(n, st_ - 1))
                    else:
                        e.wait_ge(xtev[b].sem, xtev[b].at(n, 6 * (st_ // 2) + l - 1))
                    if l < LEVELS:
                        for m in range(4):
                            ins = e.matmul(ps[0:CH, 2 * b, m * CH:(m + 1) * CH], xt_[:, m, :],
                                           pp[:, b, m, :], start=True, stop=True)
                        ins.then_inc(xm.sem, 1)
                    for m in range(4):
                        o = ps[0:CH, 2 * b + 1, m * CH:(m + 1) * CH]
                        if l == LEVELS:
                            e.matmul(o, ident_r[:, 0, :], xt_[:, m, :], start=True, stop=False)
                        ins = e.matmul(o, pp[:, b, m, :], xt_[:, m, :], start=(l < LEVELS), stop=True)
                    ins.then_inc(xtm.sem, 1)

                def state(st_, piece):
                    b, q4 = st_ % 2, st_ % 4
                    if piece == 0:
                        if st_ == 0:
                            e.wait_ge(s_init.sem, s_init.at(n, 1))
                            e.wait_ge(row_done.sem, row_done.at(n, 8))
                        else:
                            e.wait_ge(snew.sem, snew.at(n, st_))
                            e.wait_ge(oacc.sem, oacc.at(n, 2 * st_))
                        for d in range(2):
                            ins = e.matmul(ps[0:CH, 6, d * 2 * P:(d + 1) * 2 * P], qk[:, 0, cs(st_, d)],
                                           st[:, b, 2 * d:2 * d + 2, :], start=True, stop=True)
                        ins.then_inc(ksm.sem, 1)
                    elif piece == 1:
                        e.wait_ge(r_done.sem, r_done.at(n, st_ + 1))
                        e.wait_ge(tb_done.sem, tb_done.at(n, st_ + 1))
                        for m in range(4):
                            ins = e.matmul(ps[0:CH, 7, m * P:(m + 1) * P], tb[:, b, m, :], rr[:, m, :],
                                           start=True, stop=True)
                        ins.then_inc(vm.sem, 1)
                    else:
                        e.wait_ge(vn_done.sem, vn_done.at(n, st_ + 1))
                        e.wait_ge(kt_done.sem, kt_done.at(n, st_ + 1))
                        for m in range(4):
                            ins = e.matmul(ps[:, 7, m * P:(m + 1) * P], kt[:, b, m, :], vn[:, m, :],
                                           start=True, stop=True)
                        ins.then_inc(sm.sem, 1)
                        e.wait_ge(qd_done.sem, qd_done.at(n, st_ + 1))
                        e.wait_ge(qkt_done.sem, qkt_done.at(n, st_ + 1))
                        for m in range(4):
                            o = ps[:, 6, m * CH:(m + 1) * CH]
                            e.matmul(o, st[:, b, m, :], qd[:, b, m, :], start=True, stop=False)
                            ins = e.matmul(o, vn[:, m, :], qkt[:, q4, m, :], start=False, stop=True)
                        ins.then_inc(om.sem, 1)

                schedule(e, n, pre, first, level, state)
                for i in range(2):
                    e.wait_ge(sq_done.sem, sq_done.at(n, i + 3))
                    e.wait_ge(tb_done.sem, tb_done.at(n, NC))
                    for b, (t0, tn) in enumerate(PIECES):
                        ins = e.matmul(ps[:, 3 * i + b, 0:tn], c["ones"][:, :], sq[:, i, t0:t0 + tn],
                                       start=True, stop=True)
                    ins.then_inc(ssum.sem, 1)

        @block.scalar
        def _(e):
            with e.Fori(0, QK_HEADS) as n:
                e.wait_ge(pad_done.sem, pad_done.at(n, 1))

                def copy_in(j):
                    e.wait_ge(tile.sem, tile.at(n, j + 1))
                    if j >= 2:
                        e.wait_ge(taps.sem, taps.at(n, 3 * (j - 1)))
                    for src, dst in halves(ps, 3 * (j % 2), xpad[:, j % 2, 1:T + 1]):
                        e.activation(dst, src, ACT.Copy).then_inc(x_out.sem, 1)
                    e.wait_ge(x_out.sem, x_out.at(n, 2 * j + 2))
                    e.wait_ge(heads.sem, heads.at(n, 5))
                    if j >= 2:
                        e.wait_ge(o_out[j - 2].sem, o_out[j - 2].at(n, 0))
                    e.activation(dsts[j], xpad[:, j % 2, 0:T], ACT.Copy, scale=dpar[:, 0, j:j + 1]) \
                        .then_inc(tap0.sem, 1)

                def tanh(j):
                    e.wait_ge(taps.sem, taps.at(n, 3 * j + 3))
                    if j >= 2:
                        e.wait_ge(silu.sem, silu.at(n, j - 1))
                    e.activation(tht[:, j % 2, :], dsts[j], ACT.Tanh, scale=0.5).then_inc(th_done.sem, 1)

                def z(i):
                    e.wait_ge(tile.sem, tile.at(n, i + 5))
                    for src, dst in halves(ps, 3 * i, zs[:, i, :]):
                        e.activation(dst, src, ACT.Tanh, scale=0.5).then_inc(z_tanh.sem, 1)

                def turn_out(g):
                    e.wait_ge(turned.sem, turned.at(n, g + 1))
                    if g < 5:
                        dst = vrow[:, 2 * g:2 * g + 2, :, :].rearrange("p a b m -> p (a b m)")
                        e.activation(dst, ps[0:CH, 6 + g % 2, :], ACT.Copy, scale=0.5) \
                            .then_inc(row_done.sem, 1)
                    else:
                        k0, k1 = 4 * (g - 5), min(4 * (g - 4), NC)
                        dst = krow[:, k0:k1, :].rearrange("p a m -> p (a m)")
                        e.activation(dst, ps[0:CH, 6 + g % 2, 0:(k1 - k0) * P], ACT.Copy) \
                            .then_inc(row_done.sem, 1)

                def inverse_norm(i, base, **kw):
                    e.wait_ge(ssum.sem, ssum.at(n, base + i + 1))
                    for src, dst in halves(ps, 3 * i, rn[:, i, :]):
                        e.activation(dst, src, ACT.Ln, bias=c["eps"][:, 0:1], **kw).then_inc(ln_done.sem, 1)

                copy_in(0), copy_in(1), tanh(0), copy_in(2), tanh(1), copy_in(3), tanh(2), z(0), tanh(3), z(1)
                for i in range(2):
                    e.wait_ge(silu.sem, silu.at(n, i + 1))
                    e.activation(sq[:, i, :], qk[:, i, :], ACT.Square, scale=0.5).then_inc(sq_done.sem, 1)
                for g in range(5):
                    turn_out(g)
                for i in range(2):
                    inverse_norm(i, 0)
                e.wait_ge(ln_done.sem, ln_done.at(n, 4))
                for i in range(2):
                    e.activation(rn[:, i, :], rn[:, i, :], ACT.Exp, scale=-0.5,
                                 bias=c["q_bias" if i else "k_bias"][:, 0:1]).then_inc(rn_done.sem, 1)
                for g in range(5, 8):
                    turn_out(g)

                def pre(st_, l):
                    b = st_ % 2
                    if l == 3:
                        e.wait_ge(dmat.sem, dmat.at(n, st_ + 1))
                        if st_ >= 2:
                            e.wait_ge(qkt_done.sem, qkt_done.at(n, st_ - 1))
                        e.activation(ee[:, b, :, :], ps[0:CH, 4 + b, 0:m4], ACT.Exp).then_inc(e_done.sem, 1)

                def level(st_, l):
                    b = st_ % 2
                    if not 1 <= l < LEVELS:
                        return
                    e.wait_ge(xm.sem, xm.at(n, nth(st_, l - 1, 6)))
                    e.activation(xx[:, b, :, :], ps[0:CH, 2 * b, 0:m4], ACT.Copy).then_inc(xev.sem, 1)
                    if b == 0:
                        e.wait_ge(xtm.sem, xtm.at(n, nth(st_, l - 1, 7)))
                        e.activation(xt[:, b, :, :], ps[0:CH, 2 * b + 1, 0:m4], ACT.Copy) \
                            .then_inc(xtev[0].sem, 1)

                def state(st_, piece):
                    if piece == 1:
                        e.wait_ge(vm.sem, vm.at(n, st_ + 1))
                        e.activation(vn[:, :, :], ps[0:CH, 7, :], ACT.Copy).then_inc(vn_done.sem, 1)

                schedule(e, n, pre, lambda *_: None, level, state)
                e.wait_ge(oacc.sem, oacc.at(n, 2 * NC))
                e.wait_ge(snew.sem, snew.at(n, NC))
                for i in range(2):
                    e.activation(sq[:, i, :], vo[:, i, :], ACT.Square).then_inc(sq_done.sem, 1)
                for i in range(2):
                    inverse_norm(i, 2, scale=1.0 / P)
                e.wait_ge(ln_done.sem, ln_done.at(n, 8))
                for i in range(2):
                    e.activation(rn[:, i, :], rn[:, i, :], ACT.Exp, scale=-0.5).then_inc(rn_done.sem, 1)

        @block.vector
        def _(e):
            with e.Fori(0, QK_HEADS) as n:
                conv_w = par[:, 2, :].rearrange("p (j t) -> p j t", t=32)
                e.tensor_copy(dpar[:, :, 0:1], conv_w[:, :, bass.ds(n + 8, 1)])
                e.tensor_copy(dpar[:, :, 1:2], conv_w[:, :, bass.ds(n, 1)])
                e.tensor_copy(dpar[:, :, 2:4], conv_w[:, :, bass.ds(n * 2 + 16, 2)])
                for name in ("g", "tail", "gt", "beta", "eg"):
                    src = tabs[name][:, :, :, bass.ds(n * 2, 2)]
                    if name == "eg":
                        ins = e.tensor_scalar(head[name][:, :, :, :], src, -1.0, None, ALU.mult)
                    else:
                        ins = e.tensor_copy(head[name][:, :, :, :], src)
                    ins.then_inc(heads.sem, 1)
                e.wait_ge(heads.sem, heads.at(n, 5))

                def conv(j):
                    e.wait_ge(tap0.sem, tap0.at(n, j + 1))
                    conv_taps(e, dsts[j], xpad[:, j % 2, :], lambda i: dpar[:, i, j:j + 1], taps, n, 3 * j)

                def silu_of(j):
                    e.wait_ge(th_done.sem, th_done.at(n, j + 1))
                    e.scalar_tensor_tensor(dsts[j], tht[:, j % 2, :], 1.0, dsts[j], ALU.add, ALU.mult) \
                        .then_inc(silu.sem, 1)

                def z(i):
                    e.wait_ge(z_tanh.sem, z_tanh.at(n, 2 * i + 2))
                    for src, dst in halves(ps, 3 * i, zs[:, i, :]):
                        e.scalar_tensor_tensor(dst, dst, 1.0, src, ALU.add, ALU.mult).then_inc(z_out.sem, 1)

                conv(0), conv(1), silu_of(0), conv(2), silu_of(1), conv(3), silu_of(2), z(0), silu_of(3), z(1)
                for i in range(2):
                    e.wait_ge(rn_done.sem, rn_done.at(n, i + 1))
                    e.tensor_tensor(qk[:, i, :], qk[:, i, :], rn[:, i, :], ALU.mult).then_inc(normed.sem, 1)
                e.wait_ge(normed.sem, normed.at(n, 2))

                def pre(st_, l):
                    b = st_ % 2
                    if l == 1:
                        e.wait_ge(gram.sem, gram.at(n, st_ + 1))
                        e.tensor_tensor(gm[:, b].rearrange("p d k i -> p (d k i)"), ps[0:CH, 4 + b, 0:m4],
                                        c["gram_mask"][:, :, :, :].rearrange("p d k i -> p (d k i)"), ALU.mult) \
                            .then_inc(gm_done.sem, 1)
                    elif l == 4:
                        e.wait_ge(e_done.sem, e_done.at(n, st_ + 1))
                        e.wait_ge(gm_done.sem, gm_done.at(n, st_ + 1))
                        if st_ >= 4:
                            e.wait_ge(pm.sem, pm.at(n, nth(st_ - 4, 7, 8)))
                        e.tensor_tensor(D4(nh[:, st_ % 4, :, :]),
                                        gm[:, b, :, 0, :].unsqueeze(2).to_broadcast([CH, 2, 2, CH]),
                                        D4(ee[:, b, :, :]), ALU.mult).then_inc(nb_done.sem, 1)
                    elif l == 6:
                        if st_ >= 4:
                            e.wait_ge(om.sem, om.at(n, st_ - 3))
                        e.tensor_tensor(D4(qkt[:, st_ % 4, :, :]),
                                        gm[:, b, :, 1, :].unsqueeze(2).to_broadcast([CH, 2, 2, CH]),
                                        D4(ee[:, b, :, :]), ALU.mult).then_inc(qkt_done.sem, 1)

                def first(st_, l):
                    b = st_ % 2
                    e.wait_ge(pm.sem, pm.at(n, nth(st_, l, 8)))
                    if l == 0 and st_ >= 2:
                        e.wait_ge(tb_done.sem, tb_done.at(n, st_ - 1))
                    P4 = ps[0:CH, 2 * b, 0:m4].rearrange("p (m i) -> p m i", m=4)
                    if l == LEVELS:
                        e.tensor_tensor(pp[:, b, :, :], P4,
                                        c["ident"][0:CH, 0:CH].unsqueeze(1).to_broadcast([CH, 4, CH]),
                                        ALU.add).then_inc(pev.sem, 1)
                        return
                    dst = (xx if l == 0 else pp)[:, b, :, :]
                    e.tensor_tensor(D4(dst), D4(P4),
                                    c["level_mask"][:, l, :, 0:CH].unsqueeze(2).to_broadcast([CH, 2, 2, CH]),
                                    ALU.mult).then_inc(pev.sem, 1)

                def level(st_, l):
                    b = st_ % 2
                    if b == 1 and 1 <= l < LEVELS:
                        e.wait_ge(xtm.sem, xtm.at(n, nth(st_, l - 1, 7)))
                        e.tensor_copy(xt[:, b, :, :], ps[0:CH, 2 * b + 1, 0:m4]).then_inc(xtev[1].sem, 1)
                    if l < LEVELS:
                        return
                    e.wait_ge(xtm.sem, xtm.at(n, nth(st_, 6, 7)))
                    if st_ >= 2:
                        e.wait_ge(vm.sem, vm.at(n, st_ - 1))
                    e.tensor_tensor(D4(tb[:, b, :, :]),
                                    D4(ps[0:CH, 2 * b + 1, 0:m4].rearrange("p (m i) -> p m i", m=4)),
                                    head["beta"][:, :, st_, :].unsqueeze(3).to_broadcast([CH, 2, 2, CH]),
                                    ALU.mult).then_inc(tb_done.sem, 1)

                def state(st_, piece):
                    b = st_ % 2
                    if piece == 0:
                        e.wait_ge(ksm.sem, ksm.at(n, st_ + 1))
                        if st_ >= 1:
                            e.wait_ge(vm.sem, vm.at(n, st_))
                        else:
                            e.wait_ge(row_done.sem, row_done.at(n, 8))
                        for m in range(4):
                            d, r = m // 2, m % 2
                            ins = e.scalar_tensor_tensor(rr[:, m, :], ps[0:CH, 6, m * P:(m + 1) * P],
                                                         head["eg"][:, d, st_, r:r + 1],
                                                         vrow[:, chunk(st_, d), r, :], ALU.mult, ALU.add)
                        ins.then_inc(r_done.sem, 1)
                    elif piece == 2:
                        e.wait_ge(sm.sem, sm.at(n, st_ + 1))
                        if st_ == 0:
                            e.wait_ge(s_init.sem, s_init.at(n, 1))
                        else:
                            e.wait_ge(snew.sem, snew.at(n, st_))
                        for m in range(4):
                            d, r = m // 2, m % 2
                            ins = e.scalar_tensor_tensor(st[:, 1 - b, m, :], st[:, b, m, :],
                                                         head["gt"][:, d, st_, r:r + 1],
                                                         ps[:, 7, m * P:(m + 1) * P], ALU.mult, ALU.add)
                        ins.then_inc(snew.sem, 1)
                        e.wait_ge(om.sem, om.at(n, st_ + 1))
                        if st_ >= 5:
                            e.wait_ge(oacc.sem, oacc.at(n, 2 * st_))
                        for d in range(2):
                            src = ps[:, 6, d * 2 * CH:(d + 1) * 2 * CH].rearrange("p (r i) -> p r i", r=2)
                            dst = vo[:, :, cs(st_, d)]
                            if st_ < PAIRS:
                                e.tensor_copy(dst, src).then_inc(oacc.sem, 1)
                            else:
                                e.tensor_tensor(dst, dst, src, ALU.add).then_inc(oacc.sem, 1)

                schedule(e, n, pre, first, level, state)
                for i in range(2):
                    e.wait_ge(rn_done.sem, rn_done.at(n, i + 3))
                    e.scalar_tensor_tensor(vo[:, i, :], vo[:, i, :], c["half_dn_norm"][:, 0:1], rn[:, i, :],
                                           ALU.mult, ALU.mult).then_inc(scaled.sem, 1)
                    e.wait_ge(scaled.sem, scaled.at(n, i + 1))
                    e.tensor_tensor(vo[:, i, :], vo[:, i, :], zs[:, i, :], ALU.mult).then_inc(gated.sem, 1)


_OUT = (1, SEQ, D)
_INS = ["x", "meta_tokens", "norm_w", "rg_w_in", "rg_conv_w", "rg_conv_b", "rg_gate_w", "rg_gate_b",
        "rg_lambda", "rg_w_out", "dn_w_in", "dn_conv_w", "dn_a_log", "dn_dt_bias", "dn_norm_w", "dn_w_out"]


def kernel(**inputs):
    import concourse.bacc as bacc
    from concourse.bass_utils import run_bass_kernel_spmd

    nc = bacc.Bacc("TRN2", target_bir_lowering=False, num_devices=1)
    arrays, args = {}, []
    for name in _INS:
        a = np.ascontiguousarray(inputs[name])
        arrays[f"in_{name}"] = a
        args.append(nc.dram_tensor(f"in_{name}", a.shape, mybir.dt.from_np(a.dtype), kind="ExternalInput").ap())
    args.append(nc.dram_tensor("out_0", _OUT, F32, kind="ExternalOutput").ap())
    build(nc, *args)
    r = run_bass_kernel_spmd(nc, [arrays], core_ids=[0])
    return r.results[0]["out_0"]
```

```python
import math
from contextlib import ExitStack

import numpy as np

import concourse.bass as bass
from concourse import mybir

F32 = mybir.dt.float32
F32R = mybir.dt.float32r
ALU = mybir.AluOpType
ACT = mybir.ActivationFunctionType

P = 128
D = 1024
KT = D // P
SEQ, META = 1024, 16
T = SEQ + META
CH = 104
NC = T // CH
PIECES = [(0, 416), (416, 416), (832, 208)]
CPB = 4
W = 2048
WT = W // P
RG_BLOCKS = 8
QK_HEADS = 8
V_HEADS = 16
EPS = 1e-6
LEVELS = 7
UNIT = KT * P

A_CONV, A_GATEB = 0, 64
B_NORM, B_CONVB, B_LAM, B_DNNORM = 0, 32, 48, 80


class Phase(ExitStack):

    def __init__(self, nc):
        super().__init__()
        self.nc, self.sems, self.counters, self.programs = nc, [], [], ExitStack()
        self._passed = []

    def semaphore(self, name):
        self.sems.append(self.enter_context(self.nc.semaphore(name)))
        return self.sems[-1]

    @property
    def passed(self):
        if not self._passed:
            self._passed.append(self.semaphore("passed"))
        return self._passed[0]

    def counter(self, name, per=0, start=1):
        self.counters.append(Sem(self.semaphore(name), per, start))
        return self.counters[-1]

    def block(self):
        if self.counters:
            with self.nc.Block() as block:
                @block.gpsimd
                def _(e):
                    for k in self.counters:
                        e.sem_inc(k.sem, k.start)
        return self.programs.enter_context(self.nc.Block())

    def __exit__(self, *exc):
        self.programs.__exit__(*exc)
        if exc[0] is None:
            with self.nc.Block() as block:
                @block.gpsimd
                def _(e):
                    for sem in self.sems:
                        e.sem_clear(sem)
        return super().__exit__(*exc)


class Sem:

    def __init__(self, sem, per=0, start=1):
        self.sem, self.per, self.start = sem, per, start

    def at(self, n, k):
        return n * self.per + (self.start + k)


def build(nc, x, meta_tokens, norm_w, rg_w_in, rg_conv_w, rg_conv_b, rg_gate_w, rg_gate_b, rg_lambda,
          rg_w_out, dn_w_in, dn_conv_w, dn_a_log, dn_dt_bias, dn_norm_w, dn_w_out, out):
    with ExitStack() as top:
        def sb(stack, name, shape, dt=F32):
            return stack.enter_context(nc.sbuf_tensor(name, shape, dt))

        h_dram = nc.dram_tensor("h_scratch", (KT, P, T), F32, kind="Internal").ap()
        y_dram = nc.dram_tensor("y_scratch", (KT, P, T), F32, kind="Internal").ap()
        o_dram = nc.dram_tensor("o_scratch", (WT, P, T), F32, kind="Internal").ap()
        rows_dram = nc.dram_tensor("rows_scratch", (2, 2 * V_HEADS, T), F32, kind="Internal").ap()

        ps = top.enter_context(nc.psum_tensor("ps", [P, 8, 512], F32))
        c = {
            "ident": sb(top, "ident", [P, P]),
            "ones": sb(top, "ones", [P, P]),
            "upto": sb(top, "upto", [CH, 2, CH]),
            "after": sb(top, "after", [CH, 2, CH]),
            "gram_mask": sb(top, "gram_mask", [CH, 2, 2, CH]),
            "level_mask": sb(top, "level_mask", [CH, LEVELS, 2, P], mybir.dt.bfloat16),
            "par": sb(top, "par", [P, 3, P]),
            "rg_half_c": sb(top, "rg_half_c", [P, 32]),
            "rg_neg_half_c": sb(top, "rg_neg_half_c", [P, 32]),
            "rg_half_gateb": sb(top, "rg_half_gateb", [P, 64]),
            "half_dn_norm": sb(top, "half_dn_norm", [P, 1]),
            "eps": sb(top, "eps", [P, 1]),
            "q_bias": sb(top, "q_bias", [P, 1]),
            "k_bias": sb(top, "k_bias", [P, 1]),
        }
        with ExitStack() as s:
            yhi, ylo = sb(s, "rg_yhi", [P, KT, T], F32R), sb(s, "rg_ylo", [P, KT, T], F32R)
            with ExitStack() as s2:
                h = sb(s2, "h_first", [P, KT, T])
                setup(nc, sb, ps, c, x, meta_tokens, norm_w, rg_conv_w, rg_conv_b, rg_gate_b, rg_lambda,
                      dn_conv_w, dn_norm_w, h)
                norms(nc, sb, ps, c, "n0", h_dram, None, 0, 0, yhi, ylo, h=h)
            rg_loop(nc, sb, ps, c, yhi, ylo, rg_w_in, rg_gate_w, o_dram)
        out_projection(nc, sb, ps, "rgo", rg_w_out, o_dram, y_dram)
        with ExitStack() as s:
            yhi, ylo = sb(s, "dn_yhi", [P, KT, T], F32R), sb(s, "dn_ylo", [P, KT, T], F32R)
            norms(nc, sb, ps, c, "n1", h_dram, y_dram, 1, 2, yhi, ylo)
            with ExitStack() as s2:
                t = {
                    "g": sb(s2, "g", [CH, 2, NC, 16]), "beta": sb(s2, "beta", [CH, 2, NC, 16]),
                    "eg": sb(s2, "eg", [CH, 2, NC, 16]), "tail": sb(s2, "tail", [CH, 2, NC, 16]),
                    "gt": sb(s2, "gt", [P, 2, NC, 16]),
                }
                dn_tables(nc, sb, ps, c, t, yhi, ylo, dn_w_in, dn_a_log, dn_dt_bias, rows_dram)
                dn_loop(nc, sb, ps, c, t, yhi, ylo, dn_w_in, rows_dram, o_dram)
        out_projection(nc, sb, ps, "dno", dn_w_out, o_dram, y_dram)
        norms(nc, sb, ps, c, "n2", h_dram, y_dram, 3, None, None, None, out)


def setup(nc, sb, ps, c, x, meta_tokens, norm_w, rg_conv_w, rg_conv_b, rg_gate_b, rg_lambda,
          dn_conv_w, dn_norm_w, ht):
    with Phase(nc) as s:
        prow = sb(s, "prow", [P, 3, P])
        hrow = sb(s, "hrow", [CH, 2, D])
        sem = lambda n: s.semaphore(n)
        par_in, masks, par_t, par_done = sem("par_in"), sem("masks"), sem("par_t"), sem("par_done")
        row_in = [sem("row_in0"), sem("row_in1")]
        ident_ready, row_t, row_free = sem("ident_ready"), sem("row_t"), sem("row_free")
        block = s.block()

        @block.sync
        def _(e):
            loads = [
                (prow[A_CONV:A_CONV + 64, 0, :], rg_conv_w.rearrange("a j (t p) -> (a j t) p", p=P)),
                (prow[A_GATEB:A_GATEB + 64, 0, :],
                 rg_gate_b.rearrange("a d g n (t p) -> (a d g n t) p", p=P)),
                (prow[B_NORM:B_NORM + 32, 1, :], norm_w.rearrange("a b (k p) -> (a b k) p", p=P)),
                (prow[B_CONVB:B_CONVB + 16, 1, :], rg_conv_b.rearrange("a (t p) -> (a t) p", p=P)),
                (prow[B_LAM:B_LAM + 32, 1, :], rg_lambda.rearrange("a d (t p) -> (a d t) p", p=P)),
                (prow[B_DNNORM:B_DNNORM + 1, 1, :], dn_norm_w),
                (prow[:, 2, :], dn_conv_w.rearrange("a j (t p) -> (a j t) p", p=P)),
            ]
            for dst, src in loads:
                e.dma_start(dst, src).then_inc(par_in, 16)
            for k in range(NC):
                if k >= 2:
                    e.wait_ge(row_t, k - 1)
                if k == 0:
                    e.dma_start(hrow[0:META, 0, :], meta_tokens).then_inc(row_in[0], 16)
                    e.dma_start(hrow[META:CH, 0, :], x[0, 0:CH - META, :]).then_inc(row_in[0], 16)
                else:
                    e.dma_start(hrow[:, k % 2, :], x[0, k * CH - META:(k + 1) * CH - META, :]) \
                        .then_inc(row_in[k % 2], 16)

        @block.gpsimd
        def _(e):
            count = [0]

            def then(ins):
                count[0] += 1
                ins.then_inc(masks, 1)
                e.wait_ge(masks, count[0])

            def select(view, op, fill, base, ch, pattern):
                then(e.affine_select(out=view, in_=view, compare_op=op, fill=fill, base=base,
                                     pattern=pattern, channel_multiplier=ch))

            then(e.memset(c["ident"][:, :], 0.0))
            e.affine_select(out=c["ident"][:, :], in_=c["ident"][:, :], compare_op=ALU.not_equal,
                            fill=1.0, base=0, pattern=[[-1, P]], channel_multiplier=1) \
                .then_inc(ident_ready, 1)
            then(e.memset(c["ones"][:, :], 1.0))
            then(e.memset(c["eps"][:, :], EPS))
            then(e.memset(c["q_bias"][:, :], math.log(0.5 / math.sqrt(P))))
            then(e.memset(c["k_bias"][:, :], math.log(0.5)))
            for m in ("upto", "after"):
                then(e.memset(c[m][:, :, :], 1.0))
            select(c["upto"][:, 0, :], ALU.is_ge, 0.0, 0, -1, [[1, CH]])
            select(c["upto"][:, 1, :], ALU.is_ge, 0.0, 0, 1, [[-1, CH]])
            select(c["after"][:, 0, :], ALU.is_gt, 0.0, 0, 1, [[-1, CH]])
            select(c["after"][:, 1, :], ALU.is_gt, 0.0, 0, -1, [[1, CH]])
            gm = c["gram_mask"]
            then(e.memset(gm[:, :, 0, :], -1.0))
            then(e.memset(gm[:, :, 1, :], 1.0))
            select(gm[:, 0, 0, :], ALU.is_gt, 0.0, 0, -1, [[1, CH]])
            select(gm[:, 1, 0, :], ALU.is_gt, 0.0, 0, 1, [[-1, CH]])
            select(gm[:, 0, 1, :], ALU.is_ge, 0.0, 0, -1, [[1, CH]])
            select(gm[:, 1, 1, :], ALU.is_ge, 0.0, 0, 1, [[-1, CH]])
            lm = c["level_mask"]
            then(e.memset(lm[:, :, :, :], 0.0))
            for l in range(LEVELS):
                m = 1 << l
                nb = P // (2 * m)
                v = [lm[:, l, d, :].rearrange("p (b h j) -> p b h j", h=2, j=m)[:, :, d, :] for d in (0, 1)]
                for d in (0, 1):
                    then(e.memset(v[d], 1.0))
                select(v[0], ALU.is_ge, 0.0, -m, 1, [[-2 * m, nb], [0, m]])
                select(v[0], ALU.is_ge, 0.0, 2 * m - 1, -1, [[2 * m, nb], [0, m]])
                select(v[1], ALU.is_ge, 0.0, 0, 1, [[-2 * m, nb], [0, m]])
                select(v[1], ALU.is_ge, 0.0, m - 1, -1, [[2 * m, nb], [0, m]])
                for d in (0, 1):
                    select(lm[:, l, d, :], ALU.not_equal, 1.0, 0, 1, [[-1, P]])

        @block.tensor
        def _(e):
            e.wait_ge(ident_ready, 1)
            e.wait_ge(par_in, 16 * 7)
            for k, rows in enumerate((P, 81, P)):
                ins = e.transpose(ps[:, 6, k * P:k * P + rows], prow[0:rows, k, :],
                                  c["ident"][0:rows, 0:rows])
            ins.then_inc(par_t, 1)
            for k in range(NC):
                slot = k % 2
                e.wait_ge(row_in[slot], 16 * (k // 2 + 1 + (slot == 0)))
                if k >= 2:
                    e.wait_ge(row_free, k - 1)
                for b in range(KT):
                    o = ps[:, 2 * slot + b // 4, (b % 4) * CH:(b % 4 + 1) * CH]
                    ins = e.transpose(o, hrow[:, slot, b * P:(b + 1) * P], c["ident"][0:CH, 0:CH])
                ins.then_inc(row_t, 1)

        @block.vector
        def _(e):
            for k in range(NC):
                e.wait_ge(row_t, k + 1)
                src = ps[:, 2 * (k % 2):2 * (k % 2) + 2, 0:4 * CH].rearrange("p a (b t) -> p a b t", t=CH)
                dst = ht[:, :, k * CH:(k + 1) * CH].rearrange("p (a b) t -> p a b t", b=4)
                e.tensor_copy(dst, src).then_inc(row_free, 1)

        @block.scalar
        def _(e):
            n = [0]

            def then(ins):
                n[0] += 1
                ins.then_inc(par_done, 1)
                e.wait_ge(par_done, n[0])

            e.wait_ge(par_t, 1)
            e.wait_ge(masks, 6)
            par = c["par"]
            then(e.activation(par[:, 0, :], ps[:, 6, 0:P], ACT.Copy))
            then(e.activation(par[:, 1, 0:81], ps[:, 6, P:P + 81], ACT.Copy))
            then(e.activation(par[:, 2, :], ps[:, 6, 2 * P:3 * P], ACT.Copy))
            e.activation(c["rg_half_gateb"][:, :], par[:, 0, A_GATEB:A_GATEB + 64], ACT.Copy, scale=0.5)
            e.activation(c["half_dn_norm"][:, :], par[:, 1, B_DNNORM:B_DNNORM + 1], ACT.Copy, scale=0.5)

    with Phase(nc) as s:
        tmp = sb(s, "sp_tmp", [P, 4, 32])
        work = sb(s, "sp_work", [P, 4, 32])
        sem = lambda n: s.semaphore(n)
        act_done, dve_done = sem("sp_act"), sem("sp_dve")
        block = s.block()
        lam = c["par"][:, 1, B_LAM:B_LAM + 32]

        @block.scalar
        def _(e):
            e.activation(tmp[:, 0, :], lam, ACT.Abs).then_inc(act_done, 1)
            e.wait_ge(act_done, 1)
            e.activation(tmp[:, 1, :], tmp[:, 0, :], ACT.Exp, scale=-1.0).then_inc(act_done, 1)
            e.activation(tmp[:, 2, :], lam, ACT.Relu, scale=-1.0).then_inc(act_done, 1)

        @block.vector
        def _(e):
            e.wait_ge(act_done, 3)
            n = softplus(e, work, tmp[:, 1, :], tmp[:, 2, :], lambda k: work[:, k, :], dve_done)
            e.tensor_scalar(c["rg_half_c"][:, :], work[:, 3, :], -4.0, None, ALU.mult)
            e.tensor_scalar(c["rg_neg_half_c"][:, :], work[:, 3, :], 4.0, None, ALU.mult) \
                .then_inc(dve_done, 1)
            e.wait_ge(dve_done, n + 1)


def softplus(e, work, expo, relu, at, done):
    n = [0]

    def then(ins):
        n[0] += 1
        ins.then_inc(done, 1)
        e.wait_ge(done, n[0])

    z, z2, p = at(0), at(1), at(2)
    then(e.tensor_scalar(z2, expo, 2.0, None, ALU.add))
    then(e.reciprocal(p, z2))
    then(e.tensor_tensor(z, expo, p, ALU.mult))
    then(e.tensor_tensor(z2, z, z, ALU.mult))
    then(e.tensor_scalar(p, z2, 1.0 / 15, None, ALU.mult))
    for k in (13, 11, 9, 7, 5, 3):
        then(e.scalar_tensor_tensor(p, p, 1.0 / k, z2, ALU.add, ALU.mult))
    then(e.scalar_tensor_tensor(p, p, 1.0, z, ALU.add, ALU.mult))
    then(e.scalar_tensor_tensor(at(3), p, 2.0, relu, ALU.mult, ALU.add))
    return n[0]


def norms(nc, sb, ps, c, tag, h_dram, y_dram, post, pre, yhi, ylo, out=None, h=None):
    par = c["par"]
    with Phase(nc) as s:
        ht = sb(s, tag + "_h", [P, KT, T]) if h is None else h
        yt = sb(s, tag + "_y", [P, KT, T]) if y_dram is not None else None
        sq = sb(s, tag + "_sq", [P, 2, T])
        rn = sb(s, tag + "_rn", [P, 2, T])
        tmp = sb(s, tag + "_tmp", [P, 4, T]) if pre is not None else None
        orow = sb(s, tag + "_orow", [CH, 2, D]) if out is not None else None
        sem = lambda n: s.semaphore(tag + n)
        h_in = [sem(f"h_in{k}") for k in range(KT)]
        y_in = [sem(f"y_in{k}") for k in range(KT)]
        squared, summed, ln_done, rn_done = sem("squared"), sem("summed"), sem("ln"), sem("rn")
        added, scaled, stored, hi_done, lo_pool, lo_dve = (
            sem(x) for x in ("added", "scaled", "stored", "hi", "lo_pool", "lo_dve"))
        term = sem("term")
        turned, row_done, out_done = sem("turned"), sem("row_done"), [sem("out0"), sem("out1")]
        block = s.block()
        rounds = ([yt] if yt is not None else []) + ([ht] if pre is not None else [])

        @block.sync
        def _(e):
            for k in range(KT):
                if yt is not None:
                    e.dma_start(yt[:, k, :], y_dram[k]).then_inc(y_in[k], 16)
                else:
                    e.dma_start(h_dram[k], ht[:, k, :]).then_inc(stored, 16)
            for k in range(KT) if yt is not None else ():
                e.dma_start(ht[:, k, :], h_dram[k]).then_inc(h_in[k], 16)
            if yt is None:
                e.wait_ge(stored, 16 * KT)
            elif pre is not None:
                for k in range(KT):
                    e.wait_ge(added, k + 1)
                    e.dma_start(h_dram[k], ht[:, k, :]).then_inc(stored, 16)
                e.wait_ge(stored, 16 * KT)
            if out is not None:
                for k in range(NC):
                    e.wait_ge(row_done, k + 1)
                    if k == 0:
                        e.dma_start(out[0, 0:CH - META, :], orow[META:CH, 0, :]).then_inc(out_done[0], 16)
                    else:
                        e.dma_start(out[0, k * CH - META:(k + 1) * CH - META, :], orow[:, k % 2, :]) \
                            .then_inc(out_done[k % 2], 16)
                for b in (0, 1):
                    e.wait_ge(out_done[b], 16 * NC // 2)

        @block.scalar
        def _(e):
            for r, src in enumerate(rounds):
                for k in range(KT):
                    q = r * KT + k
                    if src is yt:
                        e.wait_ge(y_in[k], 16)
                    elif yt is not None:
                        e.wait_ge(added, k + 1)
                    if q >= 2:
                        e.wait_ge(summed, q - 1)
                    e.activation(sq[:, q % 2, :], src[:, k, :], ACT.Square).then_inc(squared, 1)
                e.wait_ge(summed, (r + 1) * KT)
                for src_, dst in halves(ps, 3 * r, rn[:, r, :]):
                    e.activation(dst, src_, ACT.Ln, scale=1.0 / D, bias=c["eps"][:, 0:1]).then_inc(ln_done, 1)
                e.wait_ge(ln_done, 2 * (r + 1))
                e.activation(rn[:, r, :], rn[:, r, :], ACT.Exp, scale=-0.5).then_inc(rn_done, 1)
                if src is ht:
                    for k in range(KT):
                        e.wait_ge(scaled, k + 1)
                        e.activation(yhi[:, k, :], tmp[:, k % 4, :], ACT.Copy).then_inc(hi_done, 1)

        @block.tensor
        def _(e):
            for r in range(len(rounds)):
                for k in range(KT):
                    e.wait_ge(squared, r * KT + k + 1)
                    for i, (t0, tn) in enumerate(PIECES):
                        ins = e.matmul(ps[:, 3 * r + i, 0:tn], c["ones"][:, :],
                                       sq[:, (r * KT + k) % 2, t0:t0 + tn],
                                       start=(k == 0), stop=(k == KT - 1))
                    ins.then_inc(summed, 1)
            if out is not None:
                for k in range(NC):
                    e.wait_ge(added, KT)
                    if k >= 2:
                        e.wait_ge(row_done, k - 1)
                    for b in range(KT):
                        ins = e.transpose(ps[0:CH, 4 + 2 * (k % 2) + b // 4, (b % 4) * P:(b % 4 + 1) * P],
                                          ht[:, b, k * CH:(k + 1) * CH], c["ident"][:, :])
                    ins.then_inc(turned, 1)

        @block.vector
        def _(e):
            for r, src in enumerate(rounds):
                e.wait_ge(rn_done, r + 1)
                w = lambda j, k: par[:, 1, B_NORM + j * KT + k:B_NORM + j * KT + k + 1]
                if src is yt:
                    for k in range(KT):
                        e.scalar_tensor_tensor(yt[:, k, :], yt[:, k, :], w(post, k), rn[:, r, :],
                                               ALU.mult, ALU.mult).then_inc(term, 1)
                        e.wait_ge(term, k + 1)
                        e.wait_ge(h_in[k], 16)
                        e.tensor_tensor(ht[:, k, :], ht[:, k, :], yt[:, k, :], ALU.add).then_inc(added, 1)
                else:
                    for k in range(KT):
                        if k % 2 == 0 and k >= 4:
                            e.wait_ge(lo_pool, k // 2 - 1)
                        e.scalar_tensor_tensor(tmp[:, k % 4, :], ht[:, k, :], w(pre, k), rn[:, r, :],
                                               ALU.mult, ALU.mult).then_inc(scaled, 1)
                        if k % 2:
                            e.wait_ge(hi_done, k + 1)
                            e.tensor_tensor(ylo[:, k, :], tmp[:, k % 4, :], yhi[:, k, :], ALU.subtract) \
                                .then_inc(lo_dve, 1)
            if out is not None:
                for k in range(NC):
                    e.wait_ge(turned, k + 1)
                    if k >= 2:
                        e.wait_ge(out_done[k % 2], 16 * (k // 2))
                    e.tensor_copy(orow[:, k % 2, :].rearrange("p (a n) -> p a n", a=2),
                                  ps[0:CH, 4 + 2 * (k % 2):6 + 2 * (k % 2), :]).then_inc(row_done, 1)

        @block.gpsimd
        def _(e):
            if pre is not None:
                for k in range(0, KT, 2):
                    e.wait_ge(hi_done, k + 1)
                    e.tensor_tensor(ylo[:, k, :], tmp[:, k % 4, :], yhi[:, k, :], ALU.subtract) \
                        .then_inc(lo_pool, 1)


def hold(e, passed):
    e.sem_inc(passed, 1)


class Weights:

    def __init__(self, nc, sb, s, tag, parts, act_units=0):
        per = len(parts)
        self.passed = s.passed
        self.parts = parts
        self.raw = sb(s, tag + "_raw", [P, 2, UNIT])
        self.hi = sb(s, tag + "_whi", [P, 2, UNIT], F32R)
        self.lo = sb(s, tag + "_wlo", [P, 2, UNIT], F32R)
        self.loaded = [s.counter(f"{tag}_w_loaded{b}", 16 * sum(parts[b::2]), 16) for b in (0, 1)]
        self.hi_done = s.counter(tag + "_w_hi", per - act_units)
        self.split = s.counter(tag + "_w_split", per, 2)

    def load(self, e, n, j, *pairs):
        e.wait_ge(self.split.sem, self.split.at(n, j - 1))
        hold(e, self.passed)
        for view, src in pairs:
            e.dma_start(view(self.raw[:, j % 2, :]), src).then_inc(self.loaded[j % 2].sem, 16)

    def wait_unit(self, e, n, j, tile, used):
        slot = j % 2
        e.wait_ge(self.loaded[slot].sem, self.loaded[slot].at(n, 16 * sum(self.parts[slot:j + 1:2])))
        e.wait_ge(tile.sem, tile.at(n, used))

    def split_unit(self, e, n, j, tile, used, hi_by_act=None):
        slot = j % 2
        self.wait_unit(e, n, j, tile, used)
        if hi_by_act:
            e.wait_ge(hi_by_act.sem, hi_by_act.at(n, j - len(self.parts) + hi_by_act.per + 1))
        else:
            hold(e, self.passed)
            e.tensor_copy(self.hi[:, slot, :], self.raw[:, slot, :]).then_inc(self.hi_done.sem, 1)
            e.wait_ge(self.hi_done.sem, self.hi_done.at(n, j + 1))
        e.tensor_tensor(self.lo[:, slot, :], self.raw[:, slot, :], self.hi[:, slot, :], ALU.subtract) \
            .then_inc(self.split.sem, 1)

    def hi_unit(self, e, n, j, tile, used, done):
        self.wait_unit(e, n, j, tile, used)
        e.activation(self.hi[:, j % 2, :], self.raw[:, j % 2, :], ACT.Copy).then_inc(done.sem, 1)


def project(e, ps, bank, wt, blocks, moving, first=True, last=True):
    end = len(blocks) - 1
    for k, ((slot, col), (mhi, mlo)) in enumerate(zip(blocks, moving)):
        whi, wlo = wt.hi[:, slot, col:col + P], wt.lo[:, slot, col:col + P]
        for i, (t0, tn) in enumerate(PIECES):
            o = ps[:, bank + i, 0:tn]
            e.matmul(o, whi, mhi[:, t0:t0 + tn], start=(first and k == 0), stop=False)
            e.matmul(o, whi, mlo[:, t0:t0 + tn], start=False, stop=False)
            ins = e.matmul(o, wlo, mhi[:, t0:t0 + tn], start=False, stop=(last and k == end))
    return ins


def halves(ps, bank, row):
    yield ps[:, bank:bank + 2, 0:416], row[:, 0:832].rearrange("p (a t) -> p a t", a=2)
    yield ps[:, bank + 2, 0:208], row[:, 832:T]


def conv_taps(e, acc, xpad, weight, sem, n, base):
    for j in (1, 2, 3):
        e.scalar_tensor_tensor(acc, xpad[:, j:j + T], weight(j), acc, ALU.mult, ALU.add) \
            .then_inc(sem.sem, 1)
        e.wait_ge(sem.sem, sem.at(n, base + j))


def rg_loop(nc, sb, ps, c, yhi, ylo, w_in, gate_w, o_dram):
    with Phase(nc) as s:
        wt = Weights(nc, sb, s, "rg", (1, 1, 1, 1, 2, 2), 2)
        xpad, xc = sb(s, "xpad", [P, 2, T + 4]), sb(s, "xc", [P, 2, T])
        xhi, xlo = sb(s, "xhi", [P, 2, T], F32R), sb(s, "xlo", [P, 2, T], F32R)
        zs = sb(s, "zs", [P, 2, T])
        a = sb(s, "a", [P, 2, 2, T])
        u = sb(s, "u", [P, 2, 2, T])
        v = sb(s, "v", [P, 2, 2, T])
        asq = sb(s, "asq", [P, T])
        apar, dpar = sb(s, "apar", [P, 2, 10]), sb(s, "dpar", [P, 3, 2])
        S = lambda name, per=0, start=1: s.counter("rg_" + name, per, start)
        tile = S("tile", 12, 5)
        gate_hi = S("gate_hi", 2)
        apar_done, dpar_done, pad_done = S("apar", 5), S("dpar", 1), S("pad")
        x_out, tap0, taps = S("x_out", 4), S("tap0", 2), S("taps", 6)
        xhi_done, xlo_done = S("xhi", 2), S("xlo", 2)
        z_tanh, z_out = S("z_tanh", 4), S("z_out", 4)
        gate_out = S("gate_out", 16, 5)
        th_done, a_done, asq_done = S("th", 4), S("a", 4), S("asq", 4)
        v_done, u_done, s_done, b_done = S("v", 4), S("u", 4), S("s", 4), S("b", 4)
        scan, osum, odone = S("scan", 4), S("osum", 2), S("odone", 2)
        o_out = [S("o_out0", 16, 16), S("o_out1", 16, 16)]
        block = s.block()
        par = c["par"]
        DT = [(d, t) for d in range(2) for t in range(2)]

        @block.sync
        def _(e):
            cols = w_in[0].rearrange("(k p) m -> p k m", p=P)

            def store(n, ahead):
                for t in range(2):
                    e.wait_ge(odone.sem, odone.at(n, t + 1 - 2 * ahead))
                    hold(e, s.passed)
                    e.dma_start(o_dram.rearrange("a p t -> p a t")[:, bass.ds((n - ahead) * 2 + t, 1), :],
                                a[:, 0, t:t + 1, :]).then_inc(o_out[t].sem, 16)

            def turn(n, first):
                for j, off in enumerate((0, P, W, W + P)):
                    wt.load(e, n, j, (lambda r: r.rearrange("p (k m) -> p k m", k=KT),
                                      cols[:, :, bass.ds(n * 256 + off, P)]))
                if not first:
                    store(n, 1)
                for d in range(2):
                    src = gate_w[0, d].rearrange("g n (t p) m -> p g (n t) m", p=P)
                    wt.load(e, n, 4 + d, *[
                        (lambda r, g=g: r.rearrange("p (g t m) -> p g t m", g=2, t=2)[:, g],
                         src[:, g, bass.ds(n * 2, 2), :]) for g in range(2)])

            turn(0, True)
            with e.Fori(1, RG_BLOCKS) as n:
                turn(n, False)
            store(RG_BLOCKS, 1)
            for t in range(2):
                e.wait_ge(o_out[t].sem, o_out[t].at(RG_BLOCKS, 0))

        @block.gpsimd
        def _(e):
            e.memset(xpad[:, :, 0:1], 0.0)
            e.memset(xpad[:, :, T + 1:T + 4], 0.0).then_inc(pad_done.sem, 1)
            with e.Fori(0, RG_BLOCKS) as n:
                for j, used in enumerate((-4, 0, 1, 2)):
                    wt.split_unit(e, n, j, tile, used)
                wt.split_unit(e, n, 4, tile, 3, gate_hi)
                for t in range(2):
                    e.wait_ge(xhi_done.sem, xhi_done.at(n, t + 1))
                    e.tensor_tensor(xlo[:, t, :], xc[:, t, :], xhi[:, t, :], ALU.subtract) \
                        .then_inc(xlo_done.sem, 1)
                wt.split_unit(e, n, 5, tile, 4, gate_hi)

        @block.tensor
        def _(e):
            rows = [(yhi[:, k, :], ylo[:, k, :]) for k in range(KT)]
            with e.Fori(0, RG_BLOCKS) as n:
                for j in range(4):
                    e.wait_ge(wt.split.sem, wt.split.at(n, j + 1))
                    if j < 2:
                        e.wait_ge(gate_out.sem, gate_out.at(n, 2 * j - 2))
                    else:
                        e.wait_ge(x_out.sem, x_out.at(n, 2 * j - 2))
                    project(e, ps, 3 * (j % 2), wt, [(j % 2, k * P) for k in range(KT)], rows) \
                        .then_inc(tile.sem, 1)
                e.wait_ge(xlo_done.sem, xlo_done.at(n, 2))
                conv = [(xhi[:, i, :], xlo[:, i, :]) for i in range(2)]
                for q in range(8):
                    d, g, t = q // 4, q // 2 % 2, q % 2
                    if q % 4 == 0:
                        e.wait_ge(wt.split.sem, wt.split.at(n, 5 + d))
                    if q < 2:
                        e.wait_ge(z_out.sem, z_out.at(n, 2 * q + 2))
                    else:
                        e.wait_ge(gate_out.sem, gate_out.at(n, 2 * q - 2))
                    project(e, ps, 3 * (q % 2), wt, [(d, g * 512 + i * 256 + t * P) for i in range(2)],
                            conv).then_inc(tile.sem, 1)

        @block.scalar
        def _(e):
            e.wait_ge(pad_done.sem, pad_done.at(0, 1))
            pick = lambda n, src, k: src.rearrange("p (a t) -> p a t", t=WT)[:, 0:k, bass.ds(n * 2, 2)] \
                .rearrange("p a t -> p t a")
            with e.Fori(0, RG_BLOCKS) as n:
                e.wait_ge(gate_out.sem, gate_out.at(n, 0))
                e.wait_ge(a_done.sem, a_done.at(n, 0))
                col = 0
                for src, k in ((par[:, 0, A_CONV:A_CONV + 16], 1), (par[:, 1, B_CONVB:B_CONVB + 16], 1),
                               (c["rg_half_c"][:, :], 2), (c["rg_neg_half_c"][:, :], 2),
                               (c["rg_half_gateb"][:, :], 4)):
                    e.activation(apar[:, :, col:col + k], pick(n, src, k), ACT.Copy) \
                        .then_inc(apar_done.sem, 1)
                    col += k
                e.wait_ge(apar_done.sem, apar_done.at(n, 5))
                ap = lambda t, k: apar[:, t, k:k + 1]
                for t in range(2):
                    e.wait_ge(tile.sem, tile.at(n, t + 1))
                    e.wait_ge(taps.sem, taps.at(n, 0))
                    for src, dst in halves(ps, 3 * t, xpad[:, t, 1:T + 1]):
                        e.activation(dst, src, ACT.Copy).then_inc(x_out.sem, 1)
                    e.wait_ge(x_out.sem, x_out.at(n, 2 * t + 2))
                    e.wait_ge(v_done.sem, v_done.at(n, 0))
                    e.wait_ge(xlo_done.sem, xlo_done.at(n, 0))
                    e.activation(xc[:, t, :], xpad[:, t, 0:T], ACT.Identity, scale=ap(t, 0),
                                 bias=ap(t, 1)).then_inc(tap0.sem, 1)
                for t in range(2):
                    e.wait_ge(tile.sem, tile.at(n, t + 3))
                    e.wait_ge(odone.sem, odone.at(n, 0))
                    for src, dst in halves(ps, 3 * t, zs[:, t, :]):
                        e.activation(dst, src, ACT.Tanh, scale=0.5).then_inc(z_tanh.sem, 1)
                    wt.hi_unit(e, n, 4 + t, tile, 3 + t, gate_hi)
                    for i in range(2) if t == 0 else ():
                        e.wait_ge(taps.sem, taps.at(n, 3 * i + 3))
                        e.activation(xhi[:, i, :], xc[:, i, :], ACT.Copy).then_inc(xhi_done.sem, 1)
                for d in range(2):
                    for g in range(2):
                        for t in range(2):
                            q = 4 * d + 2 * g + t
                            e.wait_ge(tile.sem, tile.at(n, q + 5))
                            if q == 0:
                                for b in range(2):
                                    e.wait_ge(o_out[b].sem, o_out[b].at(n, 0))
                                e.wait_ge(scan.sem, scan.at(n, 0))
                            dst_row = (a, v)[g][:, d, t, :]
                            for src, dst in halves(ps, 3 * t, dst_row):
                                e.activation(dst, src, ACT.Tanh, scale=0.5,
                                             bias=ap(t, 6 + 2 * d + g)).then_inc(gate_out.sem, 1)
                for i, (d, t) in enumerate(DT):
                    if i == 0:
                        e.wait_ge(gate_out.sem, gate_out.at(n, 16))
                        e.wait_ge(osum.sem, osum.at(n, 0))
                    e.activation(u[:, d, t, :], a[:, d, t, :], ACT.Tanh, scale=ap(t, 4 + d),
                                 bias=ap(t, 4 + d)).then_inc(th_done.sem, 1)
                    e.wait_ge(th_done.sem, th_done.at(n, i + 1))
                    e.activation(a[:, d, t, :], a[:, d, t, :], ACT.Exp, scale=ap(t, 2 + d),
                                 bias=ap(t, 2 + d)).then_inc(a_done.sem, 1)
                    e.wait_ge(a_done.sem, a_done.at(n, i + 1))
                    e.wait_ge(u_done.sem, u_done.at(n, i))
                    e.activation(asq[:, :], a[:, d, t, :], ACT.Square).then_inc(asq_done.sem, 1)
                for i, (d, t) in enumerate(DT):
                    e.wait_ge(u_done.sem, u_done.at(n, i + 1))
                    e.activation(u[:, d, t, :], u[:, d, t, :], ACT.Sqrt).then_inc(s_done.sem, 1)

        @block.vector
        def _(e):
            with e.Fori(0, RG_BLOCKS) as n:
                e.wait_ge(taps.sem, taps.at(n, 0))
                taps_of = par[:, 0, A_CONV:A_CONV + 64].rearrange("p (j t) -> p j t", t=WT)
                e.tensor_copy(dpar[:, :, :], taps_of[:, 1:4, bass.ds(n * 2, 2)]).then_inc(dpar_done.sem, 1)
                e.wait_ge(dpar_done.sem, dpar_done.at(n, 1))
                for t in range(2):
                    e.wait_ge(tap0.sem, tap0.at(n, t + 1))
                    conv_taps(e, xc[:, t, :], xpad[:, t, :], lambda j: dpar[:, j - 1, t:t + 1], taps, n, 3 * t)
                for t in range(2):
                    e.wait_ge(z_tanh.sem, z_tanh.at(n, 2 * t + 2))
                    for src, dst in halves(ps, 3 * t, zs[:, t, :]):
                        e.scalar_tensor_tensor(dst, dst, 1.0, src, ALU.add, ALU.mult) \
                            .then_inc(z_out.sem, 1)
                for i, (d, t) in enumerate(DT):
                    e.wait_ge(gate_out.sem, gate_out.at(n, 2 * (4 * d + 2 + t) + 2))
                    e.scalar_tensor_tensor(v[:, d, t, :], v[:, d, t, :], 1.0, xc[:, t, :],
                                           ALU.add, ALU.mult).then_inc(v_done.sem, 1)
                for i, (d, t) in enumerate(DT):
                    e.wait_ge(asq_done.sem, asq_done.at(n, i + 1))
                    e.scalar_tensor_tensor(u[:, d, t, :], asq[:, :], 1.0, u[:, d, t, :],
                                           ALU.add, ALU.mult).then_inc(u_done.sem, 1)
                for i, (d, t) in enumerate(DT):
                    e.wait_ge(s_done.sem, s_done.at(n, i + 1))
                    e.wait_ge(v_done.sem, v_done.at(n, i + 1))
                    e.scalar_tensor_tensor(v[:, d, t, :], u[:, d, t, :], 0.5, v[:, d, t, :],
                                           ALU.mult, ALU.mult).then_inc(b_done.sem, 1)
                    e.wait_ge(b_done.sem, b_done.at(n, i + 1))
                    order = slice(None) if d == 0 else slice(None, None, -1)
                    states = a[:, 0, t, :] if d == 0 else u[:, 1, t, :]
                    e.tensor_tensor_scan(states[:, order], a[:, d, t, order], v[:, d, t, order], 0.0,
                                         ALU.mult, ALU.add).then_inc(scan.sem, 1)
                for t in range(2):
                    e.wait_ge(scan.sem, scan.at(n, 3 + t))
                    e.tensor_tensor(a[:, 0, t, :], a[:, 0, t, :], u[:, 1, t, :], ALU.add) \
                        .then_inc(osum.sem, 1)
                for t in range(2):
                    e.wait_ge(osum.sem, osum.at(n, t + 1))
                    e.scalar_tensor_tensor(a[:, 0, t, :], a[:, 0, t, :], 0.5, zs[:, t, :],
                                           ALU.mult, ALU.mult).then_inc(odone.sem, 1)


def out_projection(nc, sb, ps, tag, w_out, o_dram, y_dram):
    with Phase(nc) as s:
        ohi, olo = sb(s, tag + "_ohi", [P, WT, T], F32R), sb(s, tag + "_olo", [P, WT, T], F32R)
        oraw = sb(s, tag + "_oraw", [P, 2, T])
        wt = Weights(nc, sb, s, tag, (1, 1, 1, 1))
        yo = sb(s, tag + "_yo", [P, 2, T])
        S = lambda name, per=0, start=1: s.counter(tag + "_" + name, per, start)
        o_in = [S("o_in0", 0, 16), S("o_in1", 0, 16)]
        hi_done, lo_done = S("ohi"), S("olo")
        step = S("step", 4, 2)
        y_out = S("y_out", 4, 3)
        stored = [S("stored0", 16, 16), S("stored1", 16, 16)]
        block = s.block()
        OPU = 4

        @block.sync
        def _(e):
            src = w_out[0].rearrange("(u k p) m -> p u k m", p=P, k=OPU)

            def store(n):
                for t in range(2):
                    e.wait_ge(y_out.sem, y_out.at(n, 2 * t - 2))
                    hold(e, s.passed)
                    e.dma_start(y_dram.rearrange("a p t -> p a t")[:, bass.ds(n * 2 + t - 2, 1), :],
                                yo[:, t:t + 1, :]).then_inc(stored[t].sem, 16)

            def turn(n, first):
                for j in range(4):
                    wt.load(e, n, j, (lambda r: r.rearrange("p (k m) -> p k m", k=OPU),
                                      src[:, j, :, bass.ds(n * 2 * P, 2 * P)]))
                    if j == 1 and not first:
                        store(n)

            turn(0, True)
            with e.Fori(1, KT // 2) as n:
                turn(n, False)
            store(KT // 2)
            for t in range(2):
                e.wait_ge(stored[t].sem, stored[t].at(KT // 2, 0))

        @block.scalar
        def _(e):
            for k in range(WT):
                if k >= 2:
                    e.wait_ge(lo_done.sem, lo_done.at(0, k - 1))
                e.dma_start(oraw[:, k % 2, :], o_dram[k]).then_inc(o_in[k % 2].sem, 16)
                if k >= 1:
                    e.wait_ge(o_in[(k - 1) % 2].sem, o_in[0].at(0, 16 * ((k - 1) // 2 + 1)))
                    e.activation(ohi[:, k - 1, :], oraw[:, (k - 1) % 2, :], ACT.Copy) \
                        .then_inc(hi_done.sem, 1)
            e.wait_ge(o_in[1].sem, o_in[1].at(0, 16 * WT // 2))
            e.activation(ohi[:, WT - 1, :], oraw[:, 1, :], ACT.Copy).then_inc(hi_done.sem, 1)
            with e.Fori(0, KT // 2) as n:
                for t in range(2):
                    e.wait_ge(step.sem, step.at(n, 4))
                    e.wait_ge(stored[t].sem, stored[t].at(n, 0))
                    for src, dst in halves(ps, 3 * t, yo[:, t, :]):
                        e.activation(dst, src, ACT.Copy).then_inc(y_out.sem, 1)

        @block.vector
        def _(e):
            for k in range(WT):
                e.wait_ge(hi_done.sem, hi_done.at(0, k + 1))
                e.tensor_tensor(olo[:, k, :], oraw[:, k % 2, :], ohi[:, k, :], ALU.subtract) \
                    .then_inc(lo_done.sem, 1)

        @block.gpsimd
        def _(e):
            with e.Fori(0, KT // 2) as n:
                for j in range(4):
                    wt.split_unit(e, n, j, step, j - 1)

        @block.tensor
        def _(e):
            def turn(n, first):
                for j in range(4):
                    e.wait_ge(wt.split.sem, wt.split.at(n, j + 1))
                    for i in range(OPU):
                        k = OPU * j + i
                        if first:
                            e.wait_ge(lo_done.sem, lo_done.at(0, k + 1))
                        for t in range(2):
                            if k == 0:
                                e.wait_ge(y_out.sem, y_out.at(n, 2 * t - 2))
                            ins = project(e, ps, 3 * t, wt, [(j % 2, i * 2 * P + t * P)],
                                          [(ohi[:, k, :], olo[:, k, :])], k == 0, k == WT - 1)
                    ins.then_inc(step.sem, 1)
            turn(0, True)
            with e.Fori(1, KT // 2) as n:
                turn(n, False)


def dn_tables(nc, sb, ps, c, t, yhi, ylo, w_in, a_log, dt_bias, rows_dram):
    AB = 4 * V_HEADS
    HD = 2 * V_HEADS
    off = 3 * W
    with Phase(nc) as s:
        wraw = sb(s, "ab_raw", [P, KT, AB])
        whi, wlo = sb(s, "ab_hi", [P, KT, AB], F32R), sb(s, "ab_lo", [P, KT, AB], F32R)
        consts = sb(s, "ab_consts", [CH, 3, HD])
        xa, ex, rl = sb(s, "ab_x", [CH, NC, HD]), sb(s, "ab_ex", [CH, NC, HD]), sb(s, "ab_rl", [CH, NC, HD])
        work = sb(s, "ab_work", [CH, 4, NC * HD])
        btok, eg_tok = sb(s, "ab_beta", [CH, NC, HD]), sb(s, "ab_eg", [CH, NC, HD])
        rows = sb(s, "ab_rows", [HD, 2, T])
        abrow = sb(s, "ab_row", [AB, T])
        sem = lambda n: s.semaphore("ab_" + n)
        ab_rows, rows_out = sem("ab_rows"), sem("rows_out")
        w_load, c_load, w_hi, w_lo, ab, act, dve = (sem(n) for n in
                                                   ("w_load", "c_load", "w_hi", "w_lo", "ab", "act", "dve"))
        sp, sums, tabs, row_t, row_out, stored, gdone = (sem(n) for n in
                                                        ("sp", "sums", "tabs", "row_t", "row_out", "stored", "g"))
        block = s.block()

        @block.sync
        def _(e):
            e.dma_start(wraw[:, :, :], w_in[0].rearrange("(k p) m -> p k m", p=P)[:, :, off:off + AB]) \
                .then_inc(w_load, 16)
            for i, src in enumerate((dt_bias, a_log)):
                e.dma_start(consts[:, i, :], src.rearrange("a d h -> (a d h)").partition_broadcast(CH)) \
                    .then_inc(c_load, 16)
            for i in range(2):
                e.wait_ge(row_out, 3 * (i + 1))
                e.dma_start(rows_dram[i], rows[:, i, :]).then_inc(stored, 16)
            e.wait_ge(stored, 32)

        @block.gpsimd
        def _(e):
            e.wait_ge(w_load, 16)
            e.tensor_copy(whi[:, :, :], wraw[:, :, :]).then_inc(w_hi, 1)
            e.wait_ge(w_hi, 1)
            e.tensor_tensor(wlo[:, :, :], wraw[:, :, :], whi[:, :, :], ALU.subtract).then_inc(w_lo, 1)

        @block.tensor
        def _(e):
            e.wait_ge(w_lo, 1)
            for i in range(KT):
                for b, (t0, tn) in enumerate(PIECES):
                    o = ps[0:AB, 2 + b, 0:tn]
                    yh, yl = (y[:, i, t0:t0 + tn] for y in (yhi, ylo))
                    e.matmul(o, whi[:, i, :], yh, start=(i == 0), stop=False)
                    e.matmul(o, whi[:, i, :], yl, start=False, stop=False)
                    ins = e.matmul(o, wlo[:, i, :], yh, start=False, stop=(i == KT - 1))
            ins.then_inc(ab_rows, 1)
            e.wait_ge(rows_out, 2)
            for k in range(NC):
                ins = e.transpose(ps[0:CH, k // 8, (k % 8) * AB:(k % 8 + 1) * AB],
                                  abrow[:, k * CH:(k + 1) * CH], c["ident"][0:AB, 0:AB])
            ins.then_inc(ab, 1)
            e.wait_ge(gdone, 1)
            for d in range(2):
                g = t["g"][:, d, :, :]
                cols = slice(d * NC * V_HEADS, (d + 1) * NC * V_HEADS)
                e.matmul(ps[0:CH, 2, cols], c["upto"][:, d, :], g, start=True, stop=True)
                e.matmul(ps[0:CH, 3, cols], c["after"][:, d, :], g, start=True, stop=True)
                ins = e.matmul(ps[:, 4, cols], c["ones"][0:CH, :], g, start=True, stop=True)
            ins.then_inc(sums, 1)
            for i in range(2):
                if i == 0:
                    e.wait_ge(tabs, 3)
                else:
                    e.wait_ge(row_out, 3)
                for k in range(NC):
                    src = eg_tok[:, k, :] if i == 0 else btok[:, k, :]
                    ins = e.transpose(ps[0:HD, 5 + k // CPB, (k % CPB) * CH:(k % CPB + 1) * CH], src,
                                      c["ident"][0:CH, 0:CH])
                ins.then_inc(row_t, 1)

        @block.scalar
        def _(e):
            e.wait_ge(ab_rows, 1)
            for src, dst in halves(ps, 2, abrow):
                e.activation(dst, src[0:AB], ACT.Copy).then_inc(rows_out, 1)
            e.wait_ge(dve, 2)
            for k0, k1 in ((0, 8), (8, NC)):
                src = ps[0:CH, k0 // 8, 0:(k1 - k0) * AB].rearrange("p (k m) -> p k m", m=AB)
                e.activation(btok[:, k0:k1, :], src[:, :, HD:AB], ACT.Tanh, scale=0.5).then_inc(act, 1)
            e.activation(ex[:, :, :], xa[:, :, :], ACT.Abs).then_inc(act, 1)
            e.wait_ge(act, 3)
            e.activation(ex[:, :, :], ex[:, :, :], ACT.Exp, scale=-1.0).then_inc(act, 1)
            e.activation(rl[:, :, :], xa[:, :, :], ACT.Relu).then_inc(act, 1)
            e.wait_ge(c_load, 32)
            e.activation(consts[:, 2, :], consts[:, 1, :], ACT.Exp).then_inc(act, 1)
            e.wait_ge(sums, 1)
            for i, name in enumerate(("eg", "tail", "gt")):
                rows_ = P if name == "gt" else CH
                src = ps[0:rows_, 2 + i, 0:NC * HD].rearrange("p (d k h) -> p d k h", d=2, k=NC)
                e.activation(t[name][:, :, :, :], src, ACT.Exp).then_inc(tabs, 1)
                if i == 0:
                    for d in range(2):
                        order = slice(None) if d == 0 else slice(None, None, -1)
                        e.activation(eg_tok[:, order, d * V_HEADS:(d + 1) * V_HEADS], src[:, d],
                                     ACT.Exp).then_inc(tabs, 1)
            for i in range(2):
                e.wait_ge(row_t, i + 1)
                for b, (t0, tn) in enumerate(PIECES):
                    e.activation(rows[:, i, t0:t0 + tn], ps[0:HD, 5 + b, 0:tn], ACT.Copy).then_inc(row_out, 1)

        @block.vector
        def _(e):
            e.wait_ge(ab, 1)
            e.wait_ge(c_load, 32)
            for k0, k1 in ((0, 8), (8, NC)):
                src = ps[0:CH, k0 // 8, 0:(k1 - k0) * AB].rearrange("p (k m) -> p k m", m=AB)
                e.tensor_tensor(xa[:, k0:k1, :], src[:, :, 0:HD],
                                consts[:, 0, :].unsqueeze(1).to_broadcast([CH, k1 - k0, HD]), ALU.add) \
                    .then_inc(dve, 1)
            e.wait_ge(act, 6)
            flat = lambda v: v[:, :, :].rearrange("p k m -> p (k m)")
            softplus(e, work, flat(ex), flat(rl), lambda k: work[:, k, :], sp)
            for d in range(2):
                order = slice(None) if d == 0 else slice(None, None, -1)
                hd = slice(d * V_HEADS, (d + 1) * V_HEADS)
                spv = work[:, 3, :].rearrange("p (k m) -> p k m", m=HD)[:, order, hd]
                ea = consts[:, 2, hd].unsqueeze(1).to_broadcast([CH, NC, V_HEADS])
                e.scalar_tensor_tensor(t["g"][:, d, :, :], spv, -1.0, ea, ALU.mult, ALU.mult) \
                    .then_inc(dve, 1)
            e.wait_ge(dve, 4)
            e.tensor_scalar(btok[:, :, :], btok[:, :, :], 0.5, 0.5, ALU.mult, ALU.add).then_inc(gdone, 1)
            e.wait_ge(gdone, 1)
            for d in range(2):
                order = slice(None) if d == 0 else slice(None, None, -1)
                e.tensor_copy(t["beta"][:, d, :, :], btok[:, order, d * V_HEADS:(d + 1) * V_HEADS]) \
                    .then_inc(dve, 1)
            e.wait_ge(dve, 6)


def dn_loop(nc, sb, ps, c, tabs, yhi, ylo, w_in, rows_dram, o_dram):
    PAIRS = NC // 2
    VO = 4 * P
    with Phase(nc) as s:
        wt = Weights(nc, sb, s, "dn", (1,) * 6)
        qk = sb(s, "qk", [P, 2, T])
        vo = sb(s, "vo", [P, 2, T])
        vrow, krow = sb(s, "vrow", [CH, NC, 2, P]), sb(s, "krow", [CH, NC, P])
        zs = sb(s, "dzs", [P, 2, T])
        m4 = 4 * CH
        work = sb(s, "dn_work", [P, 22 * m4 + 6 * VO])
        whi, wlo = (v[0:CH, :, :].rearrange("p a b -> p (a b)") for v in (wt.hi, wt.lo))
        shape = dict(m=4, i=CH)
        nhr = whi[:, 0:4 * m4].rearrange("p (b m i) -> p b m i", **shape)
        xx = wlo[:, 0:2 * m4].rearrange("p (b m i) -> p b m i", **shape)
        xt = wlo[:, 2 * m4:4 * m4].rearrange("p (b m i) -> p b m i", **shape)
        xt1, pp = (sb(s, k, [CH, 2, 4, CH], F32R) for k in ("xt1", "pp"))
        lg = sb(s, "lg", [CH, 2, 2, 4, CH], F32R)
        after_r = sb(s, "after_r", [CH, 2, CH], F32R)
        ghl = sb(s, "ghl", [CH, 2, 2, NC * 2], F32R)
        used = [0]

        def part(rows, *shape):
            size = int(np.prod(shape))
            v = work[0:rows, used[0]:used[0] + size]
            used[0] += size
            names = "abcde"[:len(shape)]
            if len(shape) == 1:
                return v
            return v.rearrange(f"p ({' '.join(names)}) -> p {' '.join(names)}",
                               **{n: k for n, k in zip(names, shape)})

        xpad, tht = part(P, 2, T + 4), part(P, 2, T)
        sq, rn = part(P, 2, T), part(P, 2, T)
        used[0] = 0
        gm = part(CH, 2, 2, 2, CH)
        ee, tb = (part(CH, 2, 4, CH) for _ in range(2))
        nh, qkt = part(CH, 4, 4, CH), part(CH, 4, 4, CH)
        qd, bring = part(P, 2, 4, CH), part(CH, 2, 4, CH)
        kt, st = part(CH, 2, 4, P), part(P, 2, 4, P)
        rr, vn = part(CH, 4, P), part(CH, 4, P)
        head = {k: sb(s, "head_" + k, [P if k == "gt" else CH, 2, NC, 2]) for k in ("g", "eg", "tail", "gt", "beta")}
        dpar = sb(s, "dn_dpar", [P, 4, 4])
        S = lambda name, per=0, start=1: s.counter("dn_" + name, per, start)
        tile = S("tile", 6, 2)
        pad_done, heads = S("pad", 1), S("heads", 5)
        ident_r, eye_done = sb(s, "ident_r", [CH, CH], F32R), S("eye")
        x_out, tap0, taps, th_done, silu = S("x_out", 8), S("tap0", 4), S("taps", 12), S("th", 4), S("silu", 4)
        z_tanh, z_out = S("z_tanh", 4), S("z_out", 4)
        sq_done, ssum, ln_done, rn_done, normed = S("sq", 4), S("ssum", 4), S("ln", 8, 3), S("rn", 4), S("normed", 2)
        turned, row_done = S("turned", 8), S("row_done", 8)
        b_in, c_in = [S(f"b_in{i}", 32 * PAIRS, 16) for i in (0, 1)], [S(f"c_in{i}", 32 * PAIRS, 16) for i in (0, 1)]
        lg_done, gram, dmat, gm_done, e_done = S("lg", NC), S("gram", NC), S("dmat", NC), S("gm", NC), S("e", NC)
        nb_done, nt_done, x1t_done, qkt_done = S("nb", NC), S("nt", 2 * NC), S("x1t", NC), S("qkt", NC)
        pm, pev = S("pm", (LEVELS + 1) * NC), S("pev", (LEVELS + 1) * NC)
        xm, xev = S("xm", 6 * NC), S("xev", 6 * NC)
        xtm, xtev, tb_done = S("xtm", 7 * NC), S("xtev", 6 * NC), S("tb", NC)
        ix_done, rb_done, g_split = S("ix", NC), S("rb", NC), S("g_split", 2)
        qd_done, kt_done, s_init = S("qd", NC), S("kt", NC), S("s_init", 1)
        ksm, r_done, vm, vn_done = S("ksm", NC), S("r", NC), S("vm", NC), S("vn", NC)
        om, sm, oacc, snew = S("om", NC), S("sm", NC), S("oacc", 2 * NC), S("snew", NC)
        scaled, gated = S("scaled", 2), S("gated", 2)
        o_out = [S("o_out0", 16, 16), S("o_out1", 16, 16)]
        block = s.block()
        par = c["par"]
        chunk = lambda st_, d: (st_ if d == 0 else NC - 1 - st_)
        cs = lambda st_, d: slice(chunk(st_, d) * CH, (chunk(st_, d) + 1) * CH)
        D4 = lambda v: v.rearrange("p (d r) i -> p d r i", d=2)
        OFF = (W // 2, 0, W, W + P, 2 * W, 2 * W + P)
        SUMS_QK = (((0, 0), (1, 0), (2, 0)), ((6, 0), (7, 0), (2, 208)))
        SUMS = (((3, 0), (4, 0), (5, 0)), ((6, 0), (7, 0), (5, 208)))
        MUL = (P, P, 2 * P, 2 * P, 2 * P, 2 * P)
        dsts = (qk[:, 0, :], qk[:, 1, :], vo[:, 0, :], vo[:, 1, :])

        def nth(st_, i, k):
            return st_ // 2 * 2 * k + 2 * i + st_ % 2 + 1

        def schedule(e, n, pre, first, level, state):
            for p in range(-1, PAIRS + 1):
                for l in range(LEVELS + 1):
                    if 0 <= p < PAIRS:
                        for st_ in (2 * p, 2 * p + 1):
                            first(st_, l)
                    if p + 1 < PAIRS:
                        for st_ in (2 * p + 2, 2 * p + 3):
                            pre(st_, l)
                    if p >= 1 and l < 6:
                        state(2 * p - 2 + l // 3, l % 3)
                    if 0 <= p < PAIRS:
                        for st_ in (2 * p, 2 * p + 1):
                            level(st_, l)

        @block.sync
        def _(e):
            cols = w_in[0].rearrange("(k p) m -> p k m", p=P)
            rows = [rows_dram[i].rearrange("(d h) t -> d h t", d=2) for i in range(2)]

            def load(n, j):
                wt.load(e, n, j, (lambda r: r.rearrange("p (k m) -> p k m", k=KT),
                                  cols[:, :, bass.ds(n * MUL[j] + OFF[j], P)]))

            def rows_of(n, i, ring, sems, free, per, st_):
                b = st_ % 2
                if st_ < 2:
                    e.wait_ge(normed.sem, normed.at(n, 2))
                else:
                    e.wait_ge(free.sem, free.at(n, per * (st_ - 1)))
                hold(e, s.passed)
                for d in range(2):
                    src = rows[i][d][bass.ds(n * 2, 2), cs(st_, d)]
                    e.dma_start(ring[:, b, 2 * d:2 * d + 2, :],
                                src.partition_broadcast(P if i == 0 else CH)).then_inc(sems[b].sem, 16)

            def turn(n, last):
                load(n, 4), load(n, 5)
                for st_ in (0, 1):
                    rows_of(n, 1, bring, b_in, nt_done, 2, st_)
                for p in range(PAIRS):
                    if p + 1 < PAIRS:
                        for st_ in (2 * p + 2, 2 * p + 3):
                            rows_of(n, 1, bring, b_in, nt_done, 2, st_)
                    for st_ in (2 * p, 2 * p + 1):
                        rows_of(n, 0, qd, c_in, om, 1, st_)
                if not last:
                    load(n + 1, 0), load(n + 1, 1), load(n + 1, 2), load(n + 1, 3)
                for r in range(2):
                    e.wait_ge(gated.sem, gated.at(n, r + 1))
                    hold(e, s.passed)
                    e.dma_start(o_dram.rearrange("a p t -> p a t")[:, bass.ds(n * 2 + r, 1), :],
                                vo[:, r:r + 1, :]).then_inc(o_out[r].sem, 16)

            load(0, 0), load(0, 1), load(0, 2), load(0, 3)
            with e.Fori(0, QK_HEADS - 1) as n:
                turn(n, False)
            turn(QK_HEADS - 1, True)
            for r in range(2):
                e.wait_ge(o_out[r].sem, o_out[r].at(QK_HEADS, 0))

        @block.gpsimd
        def _(e):
            e.tensor_copy(ident_r[:, :], c["ident"][0:CH, 0:CH])
            e.tensor_copy(after_r[:, :, :], c["after"][:, :, :]).then_inc(eye_done.sem, 1)

            def split(n, j):
                wt.split_unit(e, n, j, tile, j - 1)

            def turn(n, last):
                e.wait_ge(gated.sem, gated.at(n, 0))
                hold(e, s.passed)
                e.memset(xpad[:, :, 0:1], 0.0)
                e.memset(xpad[:, :, T + 1:T + 4], 0.0).then_inc(pad_done.sem, 1)
                for j in range(3, 6):
                    split(n, j)
                e.wait_ge(normed.sem, normed.at(n, 2))
                e.wait_ge(heads.sem, heads.at(n, 5))
                e.wait_ge(g_split.sem, g_split.at(n, 2))
                hold(e, s.passed)
                e.memset(st[:, 0, :, :], 0.0).then_inc(s_init.sem, 1)

                eye = c["ident"][0:CH, 0:CH].unsqueeze(1).to_broadcast([CH, 4, CH])

                def pre(st_, l):
                    b, q4 = st_ % 2, st_ % 4
                    if l == 0:
                        if st_ >= 2:
                            e.wait_ge(dmat.sem, dmat.at(n, st_ - 1))
                        for h in range(2):
                            ins = e.tensor_tensor(D4(lg[:, b, h, :, :]),
                                                  c["upto"][:, :, :].unsqueeze(2).to_broadcast([CH, 2, 2, CH]),
                                                  ghl[:, h, :, 2 * st_:2 * st_ + 2].bitcast(F32).unsqueeze(3)
                                                  .to_broadcast([CH, 2, 2, CH]), ALU.mult)
                        ins.then_inc(lg_done.sem, 1)
                    if l != 2 + 2 * b:
                        return
                    e.wait_ge(nb_done.sem, nb_done.at(n, st_ + 1))
                    e.wait_ge(b_in[b].sem, b_in[b].at(n, 32 * (st_ // 2 + 1)))
                    e.tensor_tensor(nh[:, q4, :, :], nh[:, q4, :, :], bring[:, b, :, :], ALU.mult) \
                        .then_inc(nt_done.sem, 1)
                    e.wait_ge(nt_done.sem, nt_done.at(n, 2 * st_ + 1))
                    if st_ >= 4:
                        e.wait_ge(pm.sem, pm.at(n, nth(st_ - 4, 6, 8)))
                    e.tensor_tensor(nhr[:, q4, :, :], nh[:, q4, :, :], eye, ALU.add).then_inc(nt_done.sem, 1)
                    e.wait_ge(nt_done.sem, nt_done.at(n, 2 * st_ + 2))
                    if st_ >= 2:
                        e.wait_ge(xtm.sem, xtm.at(n, nth(st_ - 2, 0, 7)))
                    lm0 = c["level_mask"][:, 0, :, 0:CH]
                    for d in range(2):
                        ins = e.tensor_tensor(D4(xt1[:, b, :, :])[:, d], D4(nhr[:, q4, :, :])[:, d],
                                              lm0[:, 1 - d, :].unsqueeze(1).to_broadcast([CH, 2, CH]),
                                              ALU.mult)
                    ins.then_inc(x1t_done.sem, 1)

                def state(st_, piece):
                    if piece != 0:
                        return
                    b = st_ % 2
                    e.wait_ge(c_in[b].sem, c_in[b].at(n, 32 * (st_ // 2 + 1)))
                    if st_ >= 2:
                        e.wait_ge(sm.sem, sm.at(n, st_ - 1))
                    for d in range(2):
                        ins = e.tensor_tensor(qd[:, b, 2 * d:2 * d + 2, :], qd[:, b, 2 * d:2 * d + 2, :],
                                              qk[:, 1, cs(st_, d)].unsqueeze(1).to_broadcast([P, 2, CH]),
                                              ALU.mult)
                    ins.then_inc(qd_done.sem, 1)
                    for d in range(2):
                        ins = e.tensor_tensor(kt[:, b, 2 * d:2 * d + 2, :],
                                              krow[:, chunk(st_, d), :].unsqueeze(1).to_broadcast([CH, 2, P]),
                                              head["tail"][:, d, st_, :].unsqueeze(2).to_broadcast([CH, 2, P]),
                                              ALU.mult)
                    ins.then_inc(kt_done.sem, 1)

                def level(st_, l):
                    if l != LEVELS - 1:
                        return
                    b = st_ % 2
                    e.wait_ge(xev.sem, xev.at(n, nth(st_, 5, 6)))
                    if st_ >= 2:
                        e.wait_ge(vm.sem, vm.at(n, st_ - 1))
                    e.tensor_tensor(tb[:, b, :, :], eye, xx[:, b, :, :].bitcast(F32), ALU.subtract) \
                        .then_inc(ix_done.sem, 1)

                schedule(e, n, pre, lambda *_: None, level, state)
                if not last:
                    e.wait_ge(tb_done.sem, tb_done.at(n, NC))
                    split(n + 1, 0), split(n + 1, 1), split(n + 1, 2)

            split(0, 0), split(0, 1), split(0, 2)
            with e.Fori(0, QK_HEADS - 1) as n:
                turn(n, False)
            turn(QK_HEADS - 1, True)

        @block.tensor
        def _(e):
            moving = [(yhi[:, k, :], ylo[:, k, :]) for k in range(KT)]
            e.wait_ge(eye_done.sem, eye_done.at(0, 1))

            def turn(n, last):
                def unit(j, bank):
                    e.wait_ge(wt.split.sem, wt.split.at(n, j + 1))
                    project(e, ps, bank, wt, [(j % 2, k * P) for k in range(KT)], moving) \
                        .then_inc(tile.sem, 1)

                def next_first(part):
                    if part == 0:
                        e.wait_ge(wt.split.sem, wt.split.at(n + 1, 1))
                        e.wait_ge(tb_done.sem, tb_done.at(n, NC))
                    ks = range(4 * part, 4 * part + 4)
                    ins = project(e, ps, 0, wt, [(0, k * P) for k in ks], [moving[k] for k in ks],
                                  part == 0, part == 1)
                    if part == 1:
                        ins.then_inc(tile.sem, 1)

                def sums(i, places, square):
                    e.wait_ge(sq_done.sem, sq_done.at(n, square + 1))
                    for (bank, col), (t0, tn) in zip(places, PIECES):
                        ins = e.matmul(ps[:, bank, col:col + tn], c["ones"][:, :], sq[:, i, t0:t0 + tn],
                                       start=True, stop=True)
                    ins.then_inc(ssum.sem, 1)

                def by_tokens(g):
                    if g >= 2:
                        e.wait_ge(row_done.sem, row_done.at(n, g - 1))
                    for i in range(4):
                        k = 2 * g + i // 2 if g < 5 else 4 * (g - 5) + i
                        if k < NC:
                            src = vo[:, i % 2, k * CH:(k + 1) * CH] if g < 5 else qk[:, 0, k * CH:(k + 1) * CH]
                            ins = e.transpose(ps[0:CH, 6 + g % 2, i * P:(i + 1) * P], src, c["ident"][:, :])
                    ins.then_inc(turned.sem, 1)

                e.wait_ge(ln_done.sem, ln_done.at(n, 0))
                unit(1, 3)
                for j in (2, 3):
                    e.wait_ge(x_out.sem, x_out.at(n, 2 * j - 2))
                    unit(j, 3 * (j % 2))
                e.wait_ge(x_out.sem, x_out.at(n, 6))
                sums(0, SUMS_QK[0], 0)
                e.wait_ge(snew.sem, snew.at(n, 0))
                sums(1, SUMS_QK[1], 1)
                e.wait_ge(x_out.sem, x_out.at(n, 8))
                unit(4, 3)
                e.wait_ge(silu.sem, silu.at(n, 4))
                e.wait_ge(ln_done.sem, ln_done.at(n, 4))
                for g in range(5):
                    by_tokens(g)
                e.wait_ge(normed.sem, normed.at(n, 1))
                for g in range(5, 8):
                    by_tokens(g)

                def pre(st_, l):
                    b = st_ % 2
                    if l == 0:
                        if st_ < 2:
                            e.wait_ge(normed.sem, normed.at(n, 2))
                            e.wait_ge(z_out.sem, z_out.at(n, 2))
                        else:
                            e.wait_ge(e_done.sem, e_done.at(n, st_ - 1))
                        for d in range(2):
                            ins = e.matmul(ps[0:CH, 4 + b, d * 2 * CH:(d + 1) * 2 * CH], qk[:, 0, cs(st_, d)],
                                           qk[:, :, cs(st_, d)], start=True, stop=True)
                        ins.then_inc(gram.sem, 1)
                    elif l == 1:
                        e.wait_ge(lg_done.sem, lg_done.at(n, st_ + 1))
                        e.wait_ge(gm_done.sem, gm_done.at(n, st_ + 1))
                        for d in range(2):
                            o = ps[0:CH, 4 + b, d * 2 * CH:(d + 1) * 2 * CH]
                            for h in range(2):
                                ins = e.matmul(o, after_r[:, d, :], lg[:, b, h, 2 * d:2 * d + 2, :],
                                               start=(h == 0), stop=(h == 1))
                        ins.then_inc(dmat.sem, 1)
                        if st_ == 1:
                            unit(5, 0)

                def first(st_, l):
                    b, q4 = st_ % 2, st_ % 4
                    if l == 0:
                        e.wait_ge(nt_done.sem, nt_done.at(n, 2 * st_ + 2))
                        if st_ >= 2:
                            e.wait_ge(pev.sem, pev.at(n, nth(st_ - 2, 7, 8)))
                        else:
                            e.wait_ge(z_out.sem, z_out.at(n, 4))
                    elif l == 1:
                        e.wait_ge(pev.sem, pev.at(n, nth(st_, 0, 8)))
                    else:
                        e.wait_ge(xev.sem, xev.at(n, nth(st_, l - 2, 6)))
                    for m in range(4):
                        o = ps[0:CH, 2 * b, m * CH:(m + 1) * CH]
                        if l < LEVELS:
                            rhs = ident_r[:, :] if l == 0 else xx[:, b, m, :]
                            ins = e.matmul(o, nhr[:, q4, m, :], rhs, start=True, stop=True)
                        else:
                            ins = e.matmul(o, nh[:, q4, m, :], xx[:, b, m, :].bitcast(F32), start=True, stop=True)
                    ins.then_inc(pm.sem, 1)

                def level(st_, l):
                    b = st_ % 2
                    if l == 0:
                        return
                    xt_ = (xt1 if l == 1 else xt)[:, b]
                    e.wait_ge(pev.sem, pev.at(n, nth(st_, l, 8)))
                    if l == 1:
                        e.wait_ge(x1t_done.sem, x1t_done.at(n, st_ + 1))
                        if st_ >= 2:
                            e.wait_ge(tb_done.sem, tb_done.at(n, st_ - 1))
                    else:
                        e.wait_ge(xtev.sem, xtev.at(n, nth(st_, l - 2, 6)))
                    if l < LEVELS:
                        for m in range(4):
                            ins = e.matmul(ps[0:CH, 2 * b, m * CH:(m + 1) * CH], xt_[:, m, :],
                                           pp[:, b, m, :], start=True, stop=True)
                        ins.then_inc(xm.sem, 1)
                    for m in range(4):
                        o = ps[0:CH, 2 * b + 1, m * CH:(m + 1) * CH]
                        ins = e.matmul(o, pp[:, b, m, :], xt_[:, m, :], start=True, stop=True)
                    ins.then_inc(xtm.sem, 1)

                def state(st_, piece):
                    b, q4 = st_ % 2, st_ % 4
                    if piece == 0:
                        if st_ == 0:
                            e.wait_ge(s_init.sem, s_init.at(n, 1))
                            e.wait_ge(row_done.sem, row_done.at(n, 8))
                        else:
                            e.wait_ge(snew.sem, snew.at(n, st_))
                            e.wait_ge(oacc.sem, oacc.at(n, 2 * st_))
                        for d in range(2):
                            ins = e.matmul(ps[0:CH, 6, d * 2 * P:(d + 1) * 2 * P], qk[:, 0, cs(st_, d)],
                                           st[:, b, 2 * d:2 * d + 2, :], start=True, stop=True)
                        ins.then_inc(ksm.sem, 1)
                        if st_ == NC - 1 and not last:
                            next_first(0)
                    elif piece == 1:
                        e.wait_ge(r_done.sem, r_done.at(n, st_ + 1))
                        e.wait_ge(tb_done.sem, tb_done.at(n, st_ + 1))
                        for m in range(4):
                            ins = e.matmul(ps[0:CH, 7, m * P:(m + 1) * P], tb[:, b, m, :], rr[:, m, :],
                                           start=True, stop=True)
                        ins.then_inc(vm.sem, 1)
                        if st_ == NC - 1 and not last:
                            next_first(1)
                    else:
                        e.wait_ge(vn_done.sem, vn_done.at(n, st_ + 1))
                        e.wait_ge(kt_done.sem, kt_done.at(n, st_ + 1))
                        for m in range(4):
                            ins = e.matmul(ps[:, 7, m * P:(m + 1) * P], kt[:, b, m, :], vn[:, m, :],
                                           start=True, stop=True)
                        ins.then_inc(sm.sem, 1)
                        e.wait_ge(qd_done.sem, qd_done.at(n, st_ + 1))
                        e.wait_ge(qkt_done.sem, qkt_done.at(n, st_ + 1))
                        for m in range(4):
                            o = ps[:, 6, m * CH:(m + 1) * CH]
                            e.matmul(o, st[:, b, m, :], qd[:, b, m, :], start=True, stop=False)
                            ins = e.matmul(o, vn[:, m, :], qkt[:, q4, m, :], start=False, stop=True)
                        ins.then_inc(om.sem, 1)

                schedule(e, n, pre, first, level, state)
                e.wait_ge(tb_done.sem, tb_done.at(n, NC))
                sums(0, SUMS[0], 2), sums(1, SUMS[1], 3)

            e.wait_ge(wt.split.sem, wt.split.at(0, 1))
            project(e, ps, 0, wt, [(0, k * P) for k in range(KT)], moving).then_inc(tile.sem, 1)
            with e.Fori(0, QK_HEADS - 1) as n:
                turn(n, False)
            turn(QK_HEADS - 1, True)

        @block.scalar
        def _(e):
            with e.Fori(0, QK_HEADS) as n:
                e.wait_ge(pad_done.sem, pad_done.at(n, 1))

                def copy_in(j):
                    e.wait_ge(tile.sem, tile.at(n, j + 1))
                    if j >= 2:
                        e.wait_ge(taps.sem, taps.at(n, 3 * (j - 1)))
                    for src, dst in halves(ps, 3 * (j % 2), xpad[:, j % 2, 1:T + 1]):
                        e.activation(dst, src, ACT.Copy).then_inc(x_out.sem, 1)
                    e.wait_ge(x_out.sem, x_out.at(n, 2 * j + 2))
                    e.wait_ge(heads.sem, heads.at(n, 5))
                    if j >= 2:
                        e.wait_ge(o_out[j - 2].sem, o_out[j - 2].at(n, 0))
                    e.activation(dsts[j], xpad[:, j % 2, 0:T], ACT.Copy, scale=dpar[:, 0, j:j + 1]) \
                        .then_inc(tap0.sem, 1)

                def tanh(j):
                    e.wait_ge(taps.sem, taps.at(n, 3 * j + 3))
                    if j >= 2:
                        e.wait_ge(silu.sem, silu.at(n, j - 1))
                    e.activation(tht[:, j % 2, :], dsts[j], ACT.Tanh, scale=0.5).then_inc(th_done.sem, 1)

                def z(i):
                    e.wait_ge(tile.sem, tile.at(n, i + 5))
                    for src, dst in halves(ps, 3 - 3 * i, zs[:, i, :]):
                        e.activation(dst, src, ACT.Tanh, scale=0.5).then_inc(z_tanh.sem, 1)

                def turn_out(g):
                    e.wait_ge(turned.sem, turned.at(n, g + 1))
                    if g < 5:
                        dst = vrow[:, 2 * g:2 * g + 2, :, :].rearrange("p a b m -> p (a b m)")
                        e.activation(dst, ps[0:CH, 6 + g % 2, :], ACT.Copy, scale=0.5) \
                            .then_inc(row_done.sem, 1)
                    else:
                        k0, k1 = 4 * (g - 5), min(4 * (g - 4), NC)
                        dst = krow[:, k0:k1, :].rearrange("p a m -> p (a m)")
                        e.activation(dst, ps[0:CH, 6 + g % 2, 0:(k1 - k0) * P], ACT.Copy) \
                            .then_inc(row_done.sem, 1)

                def log_sums(i, places, count, **kw):
                    e.wait_ge(ssum.sem, ssum.at(n, count))
                    (b0, _), _, (b2, col) = places
                    for src, dst in ((ps[:, b0:b0 + 2, 0:416], rn[:, i, 0:832].rearrange("p (a t) -> p a t", a=2)),
                                     (ps[:, b2, col:col + 208], rn[:, i, 832:T])):
                        e.activation(dst, src, ACT.Ln, bias=c["eps"][:, 0:1], **kw).then_inc(ln_done.sem, 1)

                def square(i):
                    e.wait_ge(silu.sem, silu.at(n, i + 1))
                    e.activation(sq[:, i, :], qk[:, i, :], ACT.Square, scale=0.5).then_inc(sq_done.sem, 1)

                copy_in(0), copy_in(1), tanh(0), copy_in(2), tanh(1), square(0), copy_in(3), square(1)
                tanh(2), tanh(3)
                for i in range(2):
                    log_sums(i, SUMS_QK[i], 2)
                e.wait_ge(ln_done.sem, ln_done.at(n, 4))
                for i in range(2):
                    e.activation(rn[:, i, :], rn[:, i, :], ACT.Exp, scale=-0.5,
                                 bias=c["q_bias" if i else "k_bias"][:, 0:1]).then_inc(rn_done.sem, 1)
                z(0)
                for g in range(8):
                    turn_out(g)

                def pre(st_, l):
                    b = st_ % 2
                    if l == 1:
                        e.wait_ge(dmat.sem, dmat.at(n, st_ + 1))
                        if st_ >= 2:
                            e.wait_ge(qkt_done.sem, qkt_done.at(n, st_ - 1))
                        e.activation(ee[:, b, :, :], ps[0:CH, 4 + b, 0:m4], ACT.Exp).then_inc(e_done.sem, 1)
                        if st_ == 1:
                            z(1)

                def level(st_, l):
                    if not 1 <= l < LEVELS or st_ % 2 == 0:
                        return
                    for st_ in (st_ - 1, st_):
                        e.wait_ge(xm.sem, xm.at(n, nth(st_, l - 1, 6)))
                        e.activation(xx[:, st_ % 2, :, :], ps[0:CH, 2 * (st_ % 2), 0:m4], ACT.Copy) \
                            .then_inc(xev.sem, 1)
                    for st_ in (st_ - 1, st_):
                        e.wait_ge(xtm.sem, xtm.at(n, nth(st_, l - 1, 7)))
                        e.activation(xt[:, st_ % 2, :, :], ps[0:CH, 2 * (st_ % 2) + 1, 0:m4], ACT.Copy) \
                            .then_inc(xtev.sem, 1)

                def state(st_, piece):
                    if piece == 1:
                        e.wait_ge(vm.sem, vm.at(n, st_ + 1))
                        e.activation(vn[:, :, :], ps[0:CH, 7, :], ACT.Copy).then_inc(vn_done.sem, 1)

                schedule(e, n, pre, lambda *_: None, level, state)
                e.wait_ge(oacc.sem, oacc.at(n, 2 * NC))
                e.wait_ge(snew.sem, snew.at(n, NC))
                for i in range(2):
                    e.activation(sq[:, i, :], vo[:, i, :], ACT.Square).then_inc(sq_done.sem, 1)
                for i in range(2):
                    log_sums(i, SUMS[i], 4, scale=1.0 / P)
                e.wait_ge(ln_done.sem, ln_done.at(n, 8))
                for i in range(2):
                    e.activation(rn[:, i, :], rn[:, i, :], ACT.Exp, scale=-0.5).then_inc(rn_done.sem, 1)

        @block.vector
        def _(e):
            with e.Fori(0, QK_HEADS) as n:
                conv_w = par[:, 2, :].rearrange("p (j t) -> p j t", t=32)
                e.tensor_copy(dpar[:, :, 0:1], conv_w[:, :, bass.ds(n + 8, 1)])
                e.tensor_copy(dpar[:, :, 1:2], conv_w[:, :, bass.ds(n, 1)])
                e.tensor_copy(dpar[:, :, 2:4], conv_w[:, :, bass.ds(n * 2 + 16, 2)])
                for name in ("g", "tail", "gt", "beta", "eg"):
                    src = tabs[name][:, :, :, bass.ds(n * 2, 2)]
                    if name == "eg":
                        ins = e.tensor_scalar(head[name][:, :, :, :], src, -1.0, None, ALU.mult)
                    else:
                        ins = e.tensor_copy(head[name][:, :, :, :], src)
                    ins.then_inc(heads.sem, 1)
                e.wait_ge(heads.sem, heads.at(n, 5))
                g = head["g"][:, :, :, :].rearrange("p d k r -> p d (k r)")
                e.tensor_copy(ghl[:, 0, :, :], g).then_inc(g_split.sem, 1)
                e.wait_ge(g_split.sem, g_split.at(n, 1))
                e.tensor_tensor(ghl[:, 1, :, :], g, ghl[:, 0, :, :].bitcast(F32), ALU.subtract) \
                    .then_inc(g_split.sem, 1)

                def conv(j):
                    e.wait_ge(tap0.sem, tap0.at(n, j + 1))
                    conv_taps(e, dsts[j], xpad[:, j % 2, :], lambda i: dpar[:, i, j:j + 1], taps, n, 3 * j)

                def silu_of(j):
                    e.wait_ge(th_done.sem, th_done.at(n, j + 1))
                    e.scalar_tensor_tensor(dsts[j], tht[:, j % 2, :], 1.0, dsts[j], ALU.add, ALU.mult) \
                        .then_inc(silu.sem, 1)

                def z(i):
                    e.wait_ge(z_tanh.sem, z_tanh.at(n, 2 * i + 2))
                    for src, dst in halves(ps, 3 - 3 * i, zs[:, i, :]):
                        e.scalar_tensor_tensor(dst, dst, 1.0, src, ALU.add, ALU.mult).then_inc(z_out.sem, 1)

                conv(0), conv(1), silu_of(0), conv(2), silu_of(1), conv(3), silu_of(2), silu_of(3)
                for i in range(2):
                    e.wait_ge(rn_done.sem, rn_done.at(n, i + 1))
                    e.tensor_tensor(qk[:, i, :], qk[:, i, :], rn[:, i, :], ALU.mult).then_inc(normed.sem, 1)
                z(0)
                e.wait_ge(normed.sem, normed.at(n, 2))

                def pre(st_, l):
                    b = st_ % 2
                    if l == 0:
                        e.wait_ge(gram.sem, gram.at(n, st_ + 1))
                        e.tensor_tensor(gm[:, b].rearrange("p d k i -> p (d k i)"), ps[0:CH, 4 + b, 0:m4],
                                        c["gram_mask"][:, :, :, :].rearrange("p d k i -> p (d k i)"), ALU.mult) \
                            .then_inc(gm_done.sem, 1)
                    elif l == 2:
                        e.wait_ge(e_done.sem, e_done.at(n, st_ + 1))
                        e.wait_ge(gm_done.sem, gm_done.at(n, st_ + 1))
                        if st_ >= 4:
                            e.wait_ge(pm.sem, pm.at(n, nth(st_ - 4, 7, 8)))
                        e.tensor_tensor(D4(nh[:, st_ % 4, :, :]),
                                        gm[:, b, :, 0, :].unsqueeze(2).to_broadcast([CH, 2, 2, CH]),
                                        D4(ee[:, b, :, :]), ALU.mult).then_inc(nb_done.sem, 1)
                    elif l == 6:
                        if st_ >= 4:
                            e.wait_ge(om.sem, om.at(n, st_ - 3))
                        e.tensor_tensor(D4(qkt[:, st_ % 4, :, :]),
                                        gm[:, b, :, 1, :].unsqueeze(2).to_broadcast([CH, 2, 2, CH]),
                                        D4(ee[:, b, :, :]), ALU.mult).then_inc(qkt_done.sem, 1)
                        if st_ == 1:
                            z(1)

                def first(st_, l):
                    b = st_ % 2
                    e.wait_ge(pm.sem, pm.at(n, nth(st_, l, 8)))
                    if l == 0 and st_ >= 2:
                        e.wait_ge(tb_done.sem, tb_done.at(n, st_ - 1))
                    P4 = ps[0:CH, 2 * b, 0:m4].rearrange("p (m i) -> p m i", m=4)
                    if l == LEVELS:
                        e.wait_ge(ix_done.sem, ix_done.at(n, st_ + 1))
                        e.tensor_tensor(pp[:, b, :, :], P4, tb[:, b, :, :], ALU.add).then_inc(pev.sem, 1)
                        return
                    dst = (xx if l == 0 else pp)[:, b, :, :]
                    e.tensor_tensor(D4(dst), D4(P4),
                                    c["level_mask"][:, l, :, 0:CH].unsqueeze(2).to_broadcast([CH, 2, 2, CH]),
                                    ALU.mult).then_inc(pev.sem, 1)

                def level(st_, l):
                    b = st_ % 2
                    if l < LEVELS:
                        return
                    e.wait_ge(xtm.sem, xtm.at(n, nth(st_, 6, 7)))
                    e.wait_ge(pev.sem, pev.at(n, nth(st_, 7, 8)))
                    e.tensor_tensor(tb[:, b, :, :], ps[0:CH, 2 * b + 1, 0:m4].rearrange("p (m i) -> p m i", m=4),
                                    xt[:, b, :, :].bitcast(F32), ALU.add).then_inc(tb_done.sem, 1)

                def state(st_, piece):
                    b = st_ % 2
                    if piece == 0:
                        e.wait_ge(ksm.sem, ksm.at(n, st_ + 1))
                        if st_ >= 1:
                            e.wait_ge(vm.sem, vm.at(n, st_))
                        else:
                            e.wait_ge(row_done.sem, row_done.at(n, 8))
                        for m in range(4):
                            d, r = m // 2, m % 2
                            ins = e.scalar_tensor_tensor(rr[:, m, :], ps[0:CH, 6, m * P:(m + 1) * P],
                                                         head["eg"][:, d, st_, r:r + 1],
                                                         vrow[:, chunk(st_, d), r, :], ALU.mult, ALU.add)
                        ins.then_inc(rb_done.sem, 1)
                        e.wait_ge(rb_done.sem, rb_done.at(n, st_ + 1))
                        e.tensor_tensor(D4(rr[:, :, :]), D4(rr[:, :, :]),
                                        head["beta"][:, :, st_, :].unsqueeze(3).to_broadcast([CH, 2, 2, P]),
                                        ALU.mult).then_inc(r_done.sem, 1)
                    elif piece == 2:
                        e.wait_ge(sm.sem, sm.at(n, st_ + 1))
                        if st_ == 0:
                            e.wait_ge(s_init.sem, s_init.at(n, 1))
                        else:
                            e.wait_ge(snew.sem, snew.at(n, st_))
                        for m in range(4):
                            d, r = m // 2, m % 2
                            ins = e.scalar_tensor_tensor(st[:, 1 - b, m, :], st[:, b, m, :],
                                                         head["gt"][:, d, st_, r:r + 1],
                                                         ps[:, 7, m * P:(m + 1) * P], ALU.mult, ALU.add)
                        ins.then_inc(snew.sem, 1)
                        e.wait_ge(om.sem, om.at(n, st_ + 1))
                        if st_ >= 5:
                            e.wait_ge(oacc.sem, oacc.at(n, 2 * st_))
                        for d in range(2):
                            src = ps[:, 6, d * 2 * CH:(d + 1) * 2 * CH].rearrange("p (r i) -> p r i", r=2)
                            dst = vo[:, :, cs(st_, d)]
                            if st_ < PAIRS:
                                e.tensor_copy(dst, src).then_inc(oacc.sem, 1)
                            else:
                                e.tensor_tensor(dst, dst, src, ALU.add).then_inc(oacc.sem, 1)

                schedule(e, n, pre, first, level, state)
                for i in range(2):
                    e.wait_ge(rn_done.sem, rn_done.at(n, i + 3))
                    e.scalar_tensor_tensor(vo[:, i, :], vo[:, i, :], c["half_dn_norm"][:, 0:1], rn[:, i, :],
                                           ALU.mult, ALU.mult).then_inc(scaled.sem, 1)
                    e.wait_ge(scaled.sem, scaled.at(n, i + 1))
                    e.tensor_tensor(vo[:, i, :], vo[:, i, :], zs[:, i, :], ALU.mult).then_inc(gated.sem, 1)


_OUT = (1, SEQ, D)
_INS = ["x", "meta_tokens", "norm_w", "rg_w_in", "rg_conv_w", "rg_conv_b", "rg_gate_w", "rg_gate_b",
        "rg_lambda", "rg_w_out", "dn_w_in", "dn_conv_w", "dn_a_log", "dn_dt_bias", "dn_norm_w", "dn_w_out"]


def kernel(**inputs):
    import concourse.bacc as bacc
    from concourse.bass_utils import run_bass_kernel_spmd

    nc = bacc.Bacc("TRN2", target_bir_lowering=False, num_devices=1)
    arrays, args = {}, []
    for name in _INS:
        a = np.ascontiguousarray(inputs[name])
        arrays[f"in_{name}"] = a
        args.append(nc.dram_tensor(f"in_{name}", a.shape, mybir.dt.from_np(a.dtype), kind="ExternalInput").ap())
    args.append(nc.dram_tensor("out_0", _OUT, F32, kind="ExternalOutput").ap())
    build(nc, *args)
    r = run_bass_kernel_spmd(nc, [arrays], core_ids=[0])
    return r.results[0]["out_0"]
```
